# Optimizing a Trainium2 kernel written in Bass

```python
import jax, jax.numpy as jnp
from jax import lax
import numpy as np

D_MODEL = 1024
BATCH = 1
SEQ = 2048
DEPTH = 1

CHUNK = 64
D_MIX = D_MODEL
HEAD_DIM = 64
ATTN_WIDTH = D_MIX // 2
N_HEADS = ATTN_WIDTH // HEAD_DIM
N_KV_HEADS = 2
KV_GROUP = N_HEADS // N_KV_HEADS
WINDOW = 128
WINDOW_CHUNKS = WINDOW // CHUNK
POOL_WIDTH = D_MIX - ATTN_WIDTH
POOL_WINDOWS = (2, 4, 8, 16)
N_POOL_GROUPS = len(POOL_WINDOWS)
POOL_GROUP = POOL_WIDTH // N_POOL_GROUPS
D_FF = 2816
CONV_WIDTH = 3
NORM_EPS = 1e-6
NEG_INF = -1e30
Q_COLS = N_HEADS * HEAD_DIM
KV_COLS = N_KV_HEADS * HEAD_DIM
IN_WIDTH = Q_COLS + 2 * KV_COLS + POOL_WIDTH

kernel_name = "hybrid_swa_sink_pool_convglu"

def rms_norm(x, g):
    xf = x.astype(jnp.float32)
    y = xf * lax.rsqrt(jnp.mean(xf * xf, axis=-1, keepdims=True) + NORM_EPS)
    return y * g.astype(jnp.float32)

def shift_chunks(t, j):
    if j == 0:
        return t
    return jnp.concatenate([jnp.zeros_like(t[:, :j]), t[:, :-j]], axis=1)

def band(t):
    return jnp.concatenate([shift_chunks(t, j) for j in reversed(range(WINDOW_CHUNKS))], axis=2)

def sliding_window_sink_attention(q, k, v, sinks):
    B, S = q.shape[0], q.shape[1]
    nc = S // CHUNK
    q = q.reshape(B, nc, CHUNK, N_KV_HEADS, KV_GROUP, HEAD_DIM)
    kb = band(k.reshape(B, nc, CHUNK, N_KV_HEADS, HEAD_DIM))
    vb = band(v.astype(jnp.float32).reshape(B, nc, CHUNK, N_KV_HEADS, HEAD_DIM))
    scores = jnp.einsum('bnqkgd,bnskd->bnkgqs', q, kb) * (HEAD_DIM ** -0.5)
    chunk_idx = jnp.arange(nc)[:, None]
    key_offset = (WINDOW_CHUNKS - 1) - jnp.arange(WINDOW_CHUNKS * CHUNK)[None, :] // CHUNK
    valid = (chunk_idx - key_offset) >= 0
    scores = jnp.where(valid[None, :, None, None, None, :], scores, NEG_INF)
    sink = jnp.broadcast_to(sinks.astype(jnp.float32).reshape(1, 1, N_KV_HEADS, KV_GROUP, 1, 1),
                            scores.shape[:-1] + (1,))
    probs = jax.nn.softmax(jnp.concatenate([scores, sink], axis=-1), axis=-1)[..., :-1]
    out = jnp.einsum('bnkgqs,bnskd->bnqkgd', probs, vb)
    return out.reshape(B, S, Q_COLS)

def multiscale_pool(p, pool_w, pool_b, pool_scale):
    B, S = p.shape[0], p.shape[1]
    pf = p.astype(jnp.float32).reshape(B, S, N_POOL_GROUPS, POOL_GROUP)
    pos = jnp.arange(S)
    outs = []
    for g, w in enumerate(POOL_WINDOWS):
        xg = pf[:, :, g]
        cs = jnp.cumsum(xg, axis=1)
        cs_lag = jnp.pad(cs, ((0, 0), (w, 0), (0, 0)))[:, :S]
        count = jnp.minimum(pos + 1, w).astype(jnp.float32)[None, :, None]
        mixed = (cs - cs_lag) / count - xg
        outs.append(jnp.einsum('bsc,cd->bsd', mixed, pool_w[g].astype(jnp.float32))
                    + pool_b[g].astype(jnp.float32))
    return jnp.concatenate(outs, axis=-1) * pool_scale.astype(jnp.float32)

def conv_glu(h, w_up, conv_w, conv_b, w_down):
    S = h.shape[1]
    u = h @ w_up.astype(jnp.float32)
    u_pad = jnp.pad(u, ((0, 0), (CONV_WIDTH - 1, 0), (0, 0)))
    cw = conv_w.astype(jnp.float32)
    c = sum(u_pad[:, j:j + S] * cw[j] for j in range(CONV_WIDTH)) + conv_b.astype(jnp.float32)
    gate, val = jnp.split(c, 2, axis=-1)
    return (jax.nn.silu(gate) * val) @ w_down.astype(jnp.float32)

def setup_inputs(seed: int = 0) -> dict:
    key = jax.random.key(seed)
    ks = jax.random.split(key, 16)
    f32 = jnp.float32
    L = DEPTH
    nrm = lambda k, shape, s: jax.random.normal(k, shape, f32) * s
    return {
        "x": jax.random.normal(ks[0], (BATCH, SEQ, D_MODEL), f32),
        "norm1_g": 1.0 + nrm(ks[1], (L, D_MODEL), 0.05),
        "w_in": nrm(ks[2], (L, D_MODEL, IN_WIDTH), D_MODEL ** -0.5),
        "q_norm_g": 1.0 + nrm(ks[3], (L, HEAD_DIM), 0.05),
        "k_norm_g": 1.0 + nrm(ks[4], (L, HEAD_DIM), 0.05),
        "attn_sinks": nrm(ks[5], (L, N_HEADS), 0.5),
        "pool_w": nrm(ks[6], (L, N_POOL_GROUPS, POOL_GROUP, POOL_GROUP), POOL_GROUP ** -0.5),
        "pool_b": nrm(ks[7], (L, N_POOL_GROUPS, POOL_GROUP), 0.02),
        "pool_scale": 1.0 + nrm(ks[8], (L, POOL_WIDTH), 0.1),
        "w_out": nrm(ks[9], (L, D_MIX, D_MODEL), D_MIX ** -0.5),
        "norm2_g": 1.0 + nrm(ks[10], (L, D_MODEL), 0.05),
        "w_up": nrm(ks[11], (L, D_MODEL, 2 * D_FF), D_MODEL ** -0.5),
        "conv_w": nrm(ks[12], (L, CONV_WIDTH, 2 * D_FF), CONV_WIDTH ** -0.5),
        "conv_b": nrm(ks[13], (L, 2 * D_FF), 0.02),
        "w_down": nrm(ks[14], (L, D_FF, D_MODEL), D_FF ** -0.5),
    }

def reference(x, norm1_g, w_in, q_norm_g, k_norm_g, attn_sinks, pool_w, pool_b, pool_scale,
              w_out, norm2_g, w_up, conv_w, conv_b, w_down):
    B, S, _ = x.shape
    h_res = x.astype(jnp.float32)
    for l in range(DEPTH):
        h = rms_norm(h_res, norm1_g[l])
        proj = h @ w_in[l].astype(jnp.float32)
        q = proj[..., :Q_COLS].reshape(B, S, N_HEADS, HEAD_DIM)
        k = proj[..., Q_COLS:Q_COLS + KV_COLS].reshape(B, S, N_KV_HEADS, HEAD_DIM)
        v = proj[..., Q_COLS + KV_COLS:Q_COLS + 2 * KV_COLS].reshape(B, S, N_KV_HEADS, HEAD_DIM)
        p = proj[..., Q_COLS + 2 * KV_COLS:]
        q = rms_norm(q, q_norm_g[l])
        k = rms_norm(k, k_norm_g[l])
        a = sliding_window_sink_attention(q, k, v, attn_sinks[l])
        m = multiscale_pool(p, pool_w[l], pool_b[l], pool_scale[l])
        h_res = h_res + jnp.concatenate([a, m], axis=-1) @ w_out[l].astype(jnp.float32)
        h2 = rms_norm(h_res, norm2_g[l])
        h_res = h_res + conv_glu(h2, w_up[l], conv_w[l], conv_b[l], w_down[l])
    return h_res.astype(x.dtype)


_drawn_inputs = setup_inputs


def setup_inputs(seed=0):
    import zlib

    import numpy as np

    out = dict(_drawn_inputs(seed))
    spreads = {}
    factors = {'q_norm_g': 8.0, 'k_norm_g': 8.0, 'attn_sinks': 8.0, 'pool_b': 4.184, 'conv_b': 4.412}
    for name, (base, spread) in spreads.items():
        noise = np.random.default_rng([zlib.crc32(name.encode()), seed]).standard_normal(out[name].shape)
        drawn = base * np.exp(spread * noise) if base else spread * noise
        out[name] = __import__('jax').numpy.asarray(drawn.astype(out[name].dtype))
    for name, factor in factors.items():
        out[name] = (out[name] * factor).astype(out[name].dtype)
    return out
```

```python
from contextlib import ExitStack

import concourse.bass as bass
from concourse import mybir

ALU = mybir.AluOpType
ACT = mybir.ActivationFunctionType
AX = mybir.AxisListType
F32 = mybir.dt.float32
F32R = mybir.dt.float32r

P = 128
T = 512
NT = T // P
D = 1024
KT = D // P
SEQ = 2048
NB = SEQ // T
HD = 64
QC = 512
KVC = 128
FF = 2816
FT = FF // P
WINDOWS = (2, 4, 8, 16)
CARRY = 16
EPS = 1e-6
NEG = -1e30

UNIT = 1024
RAW = 2
RING = 4
GROUPS = (8, 6, 4, 4)
BASE = (0, 8, 14, 18)

ITERATION = [
    ("F", "up", (0, 8), 16), ("F", "down", (0, 0), 4), ("F", "down", (0, 1), 4),
    ("F", "up", (8, 6), 12), ("A", "norm", (0,), 0), ("F", "down", (1, 0), 3), ("F", "down", (1, 1), 3),
    ("F", "up", (14, 8), 16),
    ("A", "turn", (0,), 0), ("F", "down", (2, 0), 2),
    ("A", "pool_in", (), 4), ("A", "q_in", (), 4), ("A", "kv_in", (), 2),
    ("F", "down", (2, 1), 2), ("A", "heads", (), 0),
    ("A", "scores", (0,), 0), ("A", "scores", (1,), 0), ("F", "down", (3, 0), 2),
    ("A", "spread", (0,), 0), ("A", "scores", (2,), 0), ("A", "mix", (0,), 0),
    ("A", "spread", (1,), 0), ("A", "scores", (3,), 0), ("A", "mix", (1,), 0),
    ("A", "spread", (2,), 0), ("A", "mix", (2,), 0), ("A", "spread", (3,), 0), ("A", "mix", (3,), 0),
    ("A", "out", (0,), 4), ("A", "out", (1,), 4), ("A", "norm", (1,), 0),
    ("F", "down", (3, 1), 2), ("A", "turn", (1,), 0),
    ("F", "store", (), 0), ("A", "keep", (), 0),
]
PROLOGUE = [s for s in ITERATION if s[0] == "A"]
EPILOGUE = [s for s in ITERATION if s[0] == "F"]
N_PRO = sum(s[3] for s in PROLOGUE)
N_ITER = sum(s[3] for s in ITERATION)
N_ALL = N_PRO + (NB - 1) * N_ITER + sum(s[3] for s in EPILOGUE)
assert N_ITER % RING == 0 and N_ITER % RAW == 0

UP_BANK = {0: 0, 8: 4, 14: 0}
DOWN_BANK = {(0, 0): 4, (0, 1): 0, (1, 0): 0, (1, 1): 4, (2, 0): 0, (2, 1): 0, (3, 0): 0, (3, 1): 4}
TURN_BANK = (4, 0)
POOL_BANK, Q_BANK, KV_BANK, HEAD_BANK = 4, 0, 4, 4
SCORE_BANK = (4, 6, 0, 2)
OUT_BANK = (4, 0)

PER = dict(
    x_loaded=16, sq_done=8, rstd_step=8, rstd_done=8, xs_ready=8, turned=16, hT_hi_done=16, hT_lo_done=16,
    p_carried=4, p_copied=4, win_step=18, mix_ready=4, pool_done=4, m_copied=4, mT_step=4, mT_ready=4,
    q_done=3, q_squared=4, q_summed=4, q_step=4, q_rstd=4, q_scaled=4,
    kv_done=3, k_squared=4, k_summed=4, k_step=4, k_rstd=4, k_scaled=4, v_kept=1,
    kT_done=1, k_placed=1, kT_ready=1, qT_done=4, qT_ready=4,
    score_done=4, sm_step=12, shift_ready=4, exp_done=4, inv_ready=4, p_scaled=4,
    spread_done=4, PT_ready=4, mix_done=4, aT_hi_done=4, aT_lo_done=4,
    out_done=6, out_added=8, res_copied=1,
    u_copied=FT, halo_in=FT, halo_kept=FT, conv_step=2 * FT, conv_done=FT, tanh_done=FT, silu_step=3 * FT,
    g_ready=FT, down_done=24, y_added=32, stored=16,
)
START = dict(u_copied=2, g_ready=2)


def at(name, block, k):
    return block * PER[name] + (k + START.get(name, 0))


def bass_hybrid_block(nc, x, norm1_g, w_in, q_norm_g, k_norm_g, attn_sinks, pool_w, pool_b, pool_scale,
                      w_out, norm2_g, w_up, conv_w, conv_b, w_down, out):
    x_v = x[0].rearrange("(t p) d -> p t d", p=P)
    out_v = out[0].rearrange("(t p) d -> p t d", p=P)
    w_in_v = w_in[0].rearrange("(k p) n -> p k n", p=P)
    w_out_v = w_out[0].rearrange("(k p) n -> p k n", p=P)
    w_up_v = w_up[0].rearrange("(k p) n -> p k n", p=P)
    w_down_v = w_down[0].rearrange("(k p) n -> p k n", p=P)

    with ExitStack() as ctx:
        def sb(name, shape, dt=F32):
            return ctx.enter_context(nc.sbuf_tensor(name, shape, dt))

        def sem(name):
            return ctx.enter_context(nc.semaphore(name))

        raw = sb("raw", [P, RAW, UNIT])
        w_hi = sb("w_hi", [P, RING, UNIT], F32R)
        w_lo = sb("w_lo", [P, RING, UNIT], F32R)
        x_a = sb("x_a", [P, NT, D])
        res = sb("res", [P, NT, D])
        xs = sb("xs", [P, NT, D])
        hT_hi = sb("hT_hi", [P, KT, T], F32R)
        hT_lo = sb("hT_lo", [P, KT, T], F32R)
        g_hi = sb("g_hi", [P, 8, T], F32R)
        g_lo = sb("g_lo", [P, 8, T], F32R)
        qT = sb("qT", [P, NT, T])
        PT = sb("PT", [P, 2, 4, P])
        kT = sb("kT", [P, NT, 2, 2, HD])
        k_keep = sb("k_keep", [P, HD])
        v_odd = sb("v_odd", [P, NT, KVC])
        v_even = sb("v_even", [P, NT + 1, KVC])
        mix_hi = sb("mix_hi", [P, T], F32R)
        mix_lo = sb("mix_lo", [P, T], F32R)
        pw_hi = sb("pw_hi", [P, 4, P], F32R)
        pw_lo = sb("pw_lo", [P, 4, P], F32R)
        work = sb("work", [P, 4160])
        ub = work[:, 0:2056].rearrange("p (r s t) -> p r s t", r=2, s=2)
        cb = work[:, 2056:4104].rearrange("p (r s t) -> p r s t", r=2, s=2)
        pbuf = work[:, 0:2 * (T + CARRY)].rearrange("p (r t) -> p r t", r=2)
        sums = work[:, 1056:1056 + 2 * (T + CARRY)].rearrange("p (r t) -> p r t", r=2)
        mf = work[:, 2112:2112 + 4 * T].rearrange("p (g t) -> p g t", g=4)
        p_keep = sb("p_keep", [P, 4, CARRY])
        halo = sb("halo", [P, FT, 2, 2])
        cst = sb("cst", [P, 200])
        cw = [cst[:, 0:44], cst[:, 44:88], cst[:, 112:156]]
        cbias = cst[:, 156:200]
        gain = [cst[:, 88:96], cst[:, 96:104]]
        pbias_in, pscale = cst[:, 104:108], cst[:, 108:112]
        pbias = sb("pbias", [P, 4])
        gq = sb("gq", [P, 1])
        gk_in = sb("gk_in", [P, 1])
        gk = sb("gk", [P, 1])
        sink_row = sb("sink_row", [P, 8])
        sink = sb("sink", [P, 8])
        neg_sink = sb("neg_sink", [P, 8])
        ratio = sb("ratio", [P, 4, CARRY])
        half_neg = sb("half_neg", [P, 8])
        ident = sb("ident", [P, P])
        ss = sb("ss", [P, NT])
        rstd = sb("rstd", [P, NT])
        ss_q = sb("ss_q", [P, NT, 8])
        rs_q = sb("rs_q", [P, NT, 8])
        ss_k = sb("ss_k", [P, NT, 2])
        rs_k = sb("rs_k", [P, NT, 2])
        mx = sb("mx", [P, NT, 8])
        shift = sb("shift", [P, NT, 8])
        sink_arg = sb("sink_arg", [P, NT, 8])
        sink_exp = sb("sink_exp", [P, NT, 8])
        row_sum = sb("row_sum", [P, NT, 8])
        den = sb("den", [P, NT, 8])
        inv = sb("inv", [P, NT, 8])
        ps = ctx.enter_context(nc.psum_tensor("ps", [P, 8, 512], F32))

        S = {name: sem(name) for name in PER}
        raw_in = [sem(f"raw_in{i}") for i in range(RAW)]
        split_hi, split_lo, unit_used = sem("split_hi"), sem("split_lo"), sem("unit_used")
        const_in, const_pool, const_cleared = sem("const_in"), sem("const_pool"), sem("const_cleared")
        sp_waited, pe_waited, pool_waited = sem("sp_waited"), sem("pe_waited"), sem("pool_waited")
        const_turned, const_step, const_ready = sem("const_turned"), sem("const_step"), sem("const_ready")

        vec_rows = res[:, 0, 0:256].rearrange("p (a n) -> p a n", a=2)
        pw_in = res[:, 1, 0:512].rearrange("p (g n) -> p g n", g=4)

        def as_f32(ap):
            return ap.bitcast(F32)

        def walk(engine, stages):
            def run(order, block_f, block_a, n, u):
                for side, name, args, units in order:
                    stages[name](block_a if side == "A" else block_f, n, u, *args)
                    n, u = n + units, u + units
            run(PROLOGUE, None, 0, 0, 0)
            with engine.Fori(0, NB - 1) as it:
                run(ITERATION, it, it + 1, it * N_ITER + N_PRO, N_PRO)
            run(EPILOGUE, NB - 1, None, N_PRO + (NB - 1) * N_ITER, N_PRO)

        def last_block(b):
            return isinstance(b, int) and b == NB - 1

        def first_block(a):
            return isinstance(a, int) and a == 0

        def stages_of(**have):
            names = {s[1] for s in ITERATION}
            return {name: have.get(name, lambda *_: None) for name in names}

        CONST_IN = 14 * 16
        CONST_POOL = 7
        CONST_STEP, CONST_READY = 6, 4

        block = ctx.enter_context(nc.Block())

        @block.sync
        def _(sp):
            def load(n, u, k, src):
                r = (u + k) % RAW
                if not isinstance(n, int) or n + k >= RAW:
                    sp.wait_ge(split_lo, n + (k - RAW + 1))
                    if not isinstance(n, int):
                        sp.sem_inc(sp_waited, 1)
                sp.dma_start(raw[:, r, :].rearrange("p (k n) -> p k n", k=src.shape[1]), src).then_inc(raw_in[r], 16)

            def load_x(a):
                if not first_block(a):
                    sp.wait_ge(S["xs_ready"], at("xs_ready", a - 1, 8))
                    sp.sem_inc(sp_waited, 1)
                    sp.wait_ge(S["res_copied"], at("res_copied", a - 1, 1))
                    sp.sem_inc(sp_waited, 1)
                sp.dma_start(x_a[:], x_v[:, bass.ds(a * NT, NT), :]).then_inc(S["x_loaded"], 16)

            def up(b, n, u, f0, count):
                with sp.Fori(0, count // 2) as j:
                    for i in range(4):
                        col = j * (2 * P) + ((f0 + i // 2) * P + (i % 2) * FF)
                        load(j * 4 + n, u, i, w_up_v[:, :, bass.ds(col, P)])
                if f0 == 0 and not last_block(b):
                    load_x(b + 1)

            def down(b, n, u, g, h):
                for k in range(GROUPS[g] // 2):
                    kt = BASE[g] + 2 * k
                    load(n, u, k, w_down_v[:, kt:kt + 2, h * 512:(h + 1) * 512])

            def pool_in(a, n, u):
                for g in range(4):
                    c = QC + 2 * KVC + g * P
                    load(n, u, g, w_in_v[:, :, c:c + P])

            def q_in(a, n, u):
                for k in range(4):
                    load(n, u, k, w_in_v[:, 2 * k:2 * k + 2, 0:QC])

            def kv_in(a, n, u):
                for k in range(2):
                    load(n, u, k, w_in_v[:, 4 * k:4 * k + 4, QC:QC + 2 * KVC])

            def out_proj(a, n, u, h):
                for k in range(4):
                    kt = (4 + 2 * k) % KT
                    load(n, u, k, w_out_v[:, kt:kt + 2, h * 512:(h + 1) * 512])

            load_x(0)
            for row, a, src in [(0, 0, conv_w[0, 0]), (44, 0, conv_w[0, 1]), (88, 0, norm1_g[0]),
                                (96, 0, norm2_g[0]), (104, 0, pool_b[0].rearrange("a b -> (a b)")),
                                (108, 0, pool_scale[0]), (0, 1, conv_w[0, 2]), (44, 1, conv_b[0])]:
                v = src.rearrange("(f p) -> f p", p=P)
                sp.dma_start(vec_rows[row:row + v.shape[0], a, :], v).then_inc(const_in, 16)
            sp.dma_start(pw_in, pool_w[0].rearrange("g c d -> c g d")).then_inc(const_in, 16)
            for i in range(2):
                half = slice(i * HD, (i + 1) * HD)
                sp.dma_start(gq[half, :], q_norm_g.rearrange("o d -> d o")).then_inc(const_in, 16)
                sp.dma_start(gk_in[half, :], k_norm_g.rearrange("o d -> d o")).then_inc(const_in, 16)
            sp.dma_start(sink_row[:], attn_sinks[0:1, :].broadcast_to([P, 8])).then_inc(const_in, 16)
            walk(sp, stages_of(up=up, down=down, pool_in=pool_in, q_in=q_in, kv_in=kv_in, out=out_proj))

        @block.tensor
        def _(pe):
            def passes(out_ap, l_hi, l_lo, r_hi, r_lo, first, last):
                pe.matmul(out_ap, l_hi, r_hi, start=first, stop=False)
                pe.matmul(out_ap, l_hi, r_lo, start=False, stop=False)
                return pe.matmul(out_ap, l_lo, r_hi, start=False, stop=last)

            def by_token(n, u, units, per_unit, bank, width, left, signal, before=None):
                total = units * per_unit
                for k in range(units):
                    if before:
                        before(k)
                    pe.wait_ge(split_lo, n + (k + 1))
                    s = (u + k) % RING
                    hi = w_hi[:, s, :].rearrange("p (k n) -> p k n", k=per_unit)
                    lo = w_lo[:, s, :].rearrange("p (k n) -> p k n", k=per_unit)
                    done = k == units - 1
                    steps = [(kk, t) for kk in range(per_unit) for t in range(NT)]
                    if done:
                        steps = [(kk, t) for t in range(NT) for kk in range(per_unit)]
                    for kk, t in steps:
                        i = k * per_unit + kk
                        l_hi, l_lo = left(i, t)
                        mm = passes(ps[:, bank + t, 0:width], l_hi, l_lo, hi[:, kk, :], lo[:, kk, :],
                                    i == 0, i == total - 1)
                        if i == total - 1 and t < NT - 1:
                            mm.then_inc(S[signal], 1)
                    mm.then_inc(unit_used, 1)

            def tokens(t):
                return slice(t * P, (t + 1) * P)

            def up(b, n, u, f0, count):
                if f0 == 0:
                    pe.wait_ge(S["hT_lo_done"], at("hT_lo_done", b, 16))
                elif f0 == 8:
                    pe.wait_ge(S["y_added"], at("y_added", b, 4))
                else:
                    pe.wait_ge(S["y_added"], at("y_added", b, 12))
                if not isinstance(b, int):
                    pe.sem_inc(pe_waited, 1)
                with pe.Fori(0, count // 2) as j:
                    for i in range(2):
                        bank = UP_BANK[f0] + 2 * i
                        pe.wait_ge(S["u_copied"], at("u_copied", b, j * 2 + (f0 + i - 1)))
                        for s in range(2):
                            pe.wait_ge(split_lo, n + (j * 4 + (2 * i + s + 1)))
                            w = (u + 2 * i + s) % RING
                            for k in range(KT):
                                c = slice(k * P, (k + 1) * P)
                                mm = passes(ps[:, bank + s, :], w_hi[:, w, c], w_lo[:, w, c],
                                            hT_hi[:, k, :], hT_lo[:, k, :], k == 0, k == KT - 1)
                            mm.then_inc(unit_used, 1)

            def down(b, n, u, g, h):
                last = last_block(b)
                if (g, h) == (0, 1):
                    pe.wait_ge(S["u_copied"], at("u_copied", b, 8))
                elif (g, h) == (1, 0):
                    pe.wait_ge(S["y_added"], at("y_added", b, 8))
                elif (g, h) == (1, 1):
                    pe.wait_ge(S["u_copied"], at("u_copied", b, 14))
                elif (g, h) == (2, 0):
                    pe.wait_ge(S["u_copied"], at("u_copied", b, 22))
                elif (g, h) == (2, 1) and not last:
                    pe.wait_ge(S["q_scaled"], at("q_scaled", b + 1, 4))
                elif (g, h) == (2, 1):
                    pe.wait_ge(S["y_added"], at("y_added", b, 20))
                elif (g, h) == (3, 0):
                    pe.wait_ge(S["y_added"], at("y_added", b, 24))
                elif (g, h) == (3, 1) and not last:
                    pe.wait_ge(S["out_added"], at("out_added", b + 1, 4))
                elif (g, h) == (3, 1):
                    pe.wait_ge(S["y_added"], at("y_added", b, 16))
                slot0 = {0: 0, 1: 0, 2: 0, 3: 4}[g]
                by_token(n, u, GROUPS[g] // 2, 2, DOWN_BANK[g, h], 512,
                         lambda i, t: (g_hi[:, slot0 + i, tokens(t)], g_lo[:, slot0 + i, tokens(t)]),
                         "down_done",
                         lambda k: pe.wait_ge(S["g_ready"], at("g_ready", b, BASE[g] + 2 * k + 2)))

            def turn(a, n, u, i):
                pe.wait_ge(S["xs_ready"], at("xs_ready", a, 4 * i + 4))
                if i == 1:
                    pe.wait_ge(S["out_added"], at("out_added", a, 8))
                elif not first_block(a):
                    pe.wait_ge(S["y_added"], at("y_added", a - 1, 16))
                for dt in range(KT):
                    if dt >= 4:
                        pe.wait_ge(S["hT_lo_done"], at("hT_lo_done", a, 8 * i + dt - 3))
                    bank = TURN_BANK[i] + dt % 4
                    for t in range(NT):
                        mm = pe.transpose(ps[:, bank, tokens(t)], xs[:, t, dt * P:(dt + 1) * P], ident[:])
                    mm.then_inc(S["turned"], 1)

            def pool_in(a, n, u):
                pe.wait_ge(S["hT_lo_done"], at("hT_lo_done", a, 8))
                for g in range(4):
                    pe.wait_ge(split_lo, n + (g + 1))
                    w = (u + g) % RING
                    for k in range(KT):
                        c = slice(k * P, (k + 1) * P)
                        mm = passes(ps[:, POOL_BANK + g, :], w_hi[:, w, c], w_lo[:, w, c],
                                    hT_hi[:, k, :], hT_lo[:, k, :], k == 0, k == KT - 1)
                    mm.then_inc(unit_used, 1)

            def h_left(i, t):
                return hT_hi[:, i, tokens(t)], hT_lo[:, i, tokens(t)]

            def q_in(a, n, u):
                if first_block(a):
                    pe.wait_ge(const_ready, CONST_READY)
                else:
                    pe.wait_ge(S["y_added"], at("y_added", a - 1, 20))

                def pool_map(g):
                    pe.wait_ge(S["mix_ready"], at("mix_ready", a, g + 1))
                    pe.wait_ge(S["p_copied"], at("p_copied", a, g + 1))
                    passes(ps[:, POOL_BANK + g, :], pw_hi[:, g, :], pw_lo[:, g, :], mix_hi[:], mix_lo[:],
                           True, True).then_inc(S["pool_done"], 1)

                by_token(n, u, 4, 2, Q_BANK, QC, h_left, "q_done",
                         lambda k: pool_map(k - 2) if k >= 2 else None)
                pool_map(2)
                pool_map(3)

            def kv_in(a, n, u):
                pe.wait_ge(S["m_copied"], at("m_copied", a, 4))
                by_token(n, u, 2, 4, KV_BANK, 2 * KVC, h_left, "kv_done")

            def heads(a, n, u):
                pe.wait_ge(S["k_scaled"], at("k_scaled", a, 4))
                for t in range(NT):
                    mm = pe.transpose(ps[:, HEAD_BANK, tokens(t)], xs[:, t, QC:QC + KVC], ident[:])
                mm.then_inc(S["kT_done"], 1)
                pe.wait_ge(S["q_scaled"], at("q_scaled", a, 4))
                for t in range(NT):
                    if t == 3:
                        pe.wait_ge(S["kT_ready"], at("kT_ready", a, 1))
                    bank = HEAD_BANK + (1 + t) % 4
                    for j in range(4):
                        q_t = ps[:, bank, :].rearrange("p (c j q) -> p j c q", c=2, j=4)[:, j]
                        mm = pe.transpose(q_t, xs[:, t, j * P:(j + 1) * P], ident[:])
                    mm.then_inc(S["qT_done"], 1)

            def scores(a, n, u, t):
                if t == 0:
                    pe.wait_ge(S["qT_ready"], at("qT_ready", a, 4))
                if t == 2 and not first_block(a):
                    pe.wait_ge(S["y_added"], at("y_added", a - 1, 28))
                for v in range(2):
                    rows = slice(v * HD, (v + 1) * HD)
                    for c in range(2):
                        for j in range(2):
                            q = slice((2 * c + j) * P, (2 * c + j + 1) * P)
                            mm = pe.matmul(ps[:, SCORE_BANK[t] + v, q], qT[rows, t, q],
                                           kT[rows, t, c].rearrange("p a d -> p (a d)"), start=True, stop=True)
                mm.then_inc(S["score_done"], 1)

            def spread(a, n, u, t):
                pe.wait_ge(S["p_scaled"], at("p_scaled", a, t + 1))
                for i in range(8):
                    mm = pe.transpose(ps[:, SCORE_BANK[t] + i // 4, (i % 4) * P:(i % 4 + 1) * P],
                                      xs[:, t, i * P:(i + 1) * P], ident[:])
                mm.then_inc(S["spread_done"], 1)

            def mix(a, n, u, t):
                pe.wait_ge(S["PT_ready"], at("PT_ready", a, t + 1))
                for v in range(2):
                    d = slice(v * HD, (v + 1) * HD)
                    for c, window in enumerate((v_even, v_odd)):
                        for i in range(2):
                            q = slice(i * HD, (i + 1) * HD)
                            o = ps[q, SCORE_BANK[t], v * 256:(v + 1) * 256] \
                                .rearrange("p (j c q) -> p c j q", j=2, c=2)[:, c]
                            mm = pe.matmul(o, window[:, t, d], PT[:, v, 2 * c:2 * c + 2, q],
                                           start=True, stop=True)
                mm.then_inc(S["mix_done"], 1)

            def out_proj(a, n, u, h):
                def before(k):
                    if h == 0 and k == 0:
                        pe.wait_ge(S["mT_ready"], at("mT_ready", a, 4))
                        pe.wait_ge(S["aT_lo_done"], at("aT_lo_done", a, 2))
                    if h == 0 and k == 2:
                        pe.wait_ge(S["aT_lo_done"], at("aT_lo_done", a, 4))
                by_token(n, u, 4, 2, OUT_BANK[h], 512, lambda i, t: h_left((4 + i) % KT, t), "out_done", before)

            pe.wait_ge(const_pool, CONST_POOL)
            pe.wait_ge(const_in, CONST_IN)
            pe.transpose(ps[:, 0, 0:112], vec_rows[0:112, 0, :], ident[0:112, 0:112])
            pe.transpose(ps[:, 0, 112:200], vec_rows[0:88, 1, :], ident[0:88, 0:88]).then_inc(const_turned, 1)
            walk(pe, stages_of(up=up, down=down, turn=turn, pool_in=pool_in, q_in=q_in, kv_in=kv_in,
                               heads=heads, scores=scores, spread=spread, mix=mix, out=out_proj))

        @block.scalar
        def _(act):
            def split(n, u, k):
                m, r, s = k + RING, (u + k + RING) % RAW, (u + k + RING) % RING
                if isinstance(n, int) and n + m >= N_ALL:
                    return
                if not isinstance(n, int) or n + k >= 0:
                    act.wait_ge(unit_used, n + (k + 1))
                act.wait_ge(raw_in[r], (n + m) * (16 // RAW) + (16 - r * (16 // RAW)))
                nc.scalar.activation(w_hi[:, s, :], raw[:, r, :], ACT.Copy).then_inc(split_hi, 1)

            def tile_done(name, b, k, n, units, t):
                if t < NT - 1:
                    act.wait_ge(S[name], at(name, b, k))
                else:
                    act.wait_ge(unit_used, n + units)

            def norm(a, n, u, i):
                def square(t):
                    if i == 1:
                        act.wait_ge(S["out_added"], at("out_added", a, 4 + t + 1))
                    nc.scalar.activation(xs[:, t, :], x_a[:, t, :], ACT.Square,
                                         accum_out=ss[:, t:t + 1]).then_inc(S["sq_done"], 1)

                def scale(t):
                    act.wait_ge(S["rstd_done"], at("rstd_done", a, 4 * i + t + 1))
                    nc.scalar.activation(xs[:, t, :], x_a[:, t, :], ACT.Copy,
                                         scale=rstd[:, t:t + 1]).then_inc(S["xs_ready"], 1)

                if i == 0:
                    act.wait_ge(S["x_loaded"], at("x_loaded", a, 16))
                    if not first_block(a):
                        act.wait_ge(S["spread_done"], at("spread_done", a - 1, 4))
                for t in range(NT):
                    square(t)
                    if t:
                        scale(t - 1)
                scale(NT - 1)

            def turn(a, n, u, i):
                for dt in range(KT):
                    act.wait_ge(S["turned"], at("turned", a, 8 * i + dt + 1))
                    nc.scalar.activation(hT_hi[:, dt, :], ps[:, TURN_BANK[i] + dt % 4, :], ACT.Copy,
                                         scale=gain[i][:, dt:dt + 1]).then_inc(S["hT_hi_done"], 1)

            def pool_in(a, n, u):
                if not first_block(a):
                    act.wait_ge(S["g_ready"], at("g_ready", a - 1, FT))
                    act.wait_ge(S["halo_kept"], at("halo_kept", a - 1, FT))
                for g in range(4):
                    split(n, u, g)
                    if g < 3:
                        pool_copy(a, n, g)

            def pool_copy(a, n, g):
                if g >= 2:
                    act.wait_ge(S["mix_ready"], at("mix_ready", a, g - 1))
                act.wait_ge(unit_used, n + (g + 1))
                buf, bank = pbuf[:, g % 2, :], ps[:, POOL_BANK + g, :]
                nc.scalar.activation(buf[:, 0:CARRY], p_keep[:, g, :], ACT.Copy).then_inc(S["p_carried"], 1)
                nc.scalar.activation(buf[:, CARRY:], bank, ACT.Copy)
                act.wait_ge(S["p_carried"], at("p_carried", a, g + 1))
                nc.scalar.activation(p_keep[:, g, :], bank[:, T - CARRY:T], ACT.Copy).then_inc(S["p_copied"], 1)

            def q_in(a, n, u):
                def pooled(g):
                    act.wait_ge(S["pool_done"], at("pool_done", a, g + 1))
                    nc.scalar.activation(mf[:, g, :], ps[:, POOL_BANK + g, :], ACT.Identity,
                                         bias=pbias[:, g:g + 1], scale=pscale[:, g:g + 1]
                                         ).then_inc(S["m_copied"], 1)

                def square(t):
                    tile_done("q_done", a, t + 1, n, 4, t)
                    nc.scalar.activation(xs[:, t, 0:QC], ps[:, Q_BANK + t, :], ACT.Square
                                         ).then_inc(S["q_squared"], 1)

                split(n, u, 0)
                split(n, u, 1)
                pool_copy(a, n - 4, 3)
                pooled(0)
                split(n, u, 2)
                pooled(1)
                split(n, u, 3)
                square(0)
                square(1)
                pooled(2)
                square(2)
                square(3)
                pooled(3)

            def kv_in(a, n, u):
                split(n, u, 0)
                split(n, u, 1)
                act.wait_ge(S["v_kept"], at("v_kept", a, 1))
                for t in range(NT):
                    tile_done("kv_done", a, t + 1, n, 2, t)
                    v_in = ps[:, KV_BANK + t, KVC:2 * KVC]
                    nc.scalar.activation(v_odd[:, t, :], v_in, ACT.Copy)
                    nc.scalar.activation(v_even[0:HD, t, :], v_in[0:HD], ACT.Copy)
                    nc.scalar.activation(v_even[HD:P, t + 1, :], v_in[HD:P], ACT.Copy)
                    nc.scalar.activation(xs[:, t, QC:QC + KVC], ps[:, KV_BANK + t, 0:KVC], ACT.Square
                                         ).then_inc(S["k_squared"], 1)

            def heads(a, n, u):
                act.wait_ge(S["kT_done"], at("kT_done", a, 1))
                nc.scalar.activation(kT[:, 0, 0, 1], k_keep[:], ACT.Copy).then_inc(S["k_placed"], 1)
                by_chunk = ps[:, HEAD_BANK, :].rearrange("p (t c d) -> p t c d", t=NT, c=2)
                even, odd = by_chunk[:, :, 0, :], by_chunk[:, :, 1, :]
                for dst, src in [(kT[:, :, 0, 0], even), (kT[:, :, 1, 0], even), (kT[:, :, 1, 1], odd),
                                 (kT[:, 1:NT, 0, 1], odd[:, 0:NT - 1])]:
                    nc.scalar.activation(dst, src, ACT.Copy, scale=gk[:, 0:1])
                act.wait_ge(S["k_placed"], at("k_placed", a, 1))
                nc.scalar.activation(k_keep[:], odd[:, NT - 1], ACT.Copy, scale=gk[:, 0:1]
                                     ).then_inc(S["kT_ready"], 1)
                for t in range(NT):
                    act.wait_ge(S["qT_done"], at("qT_done", a, t + 1))
                    nc.scalar.activation(qT[:, t, :], ps[:, HEAD_BANK + (1 + t) % 4, :], ACT.Copy,
                                         scale=gq[:, 0:1]).then_inc(S["qT_ready"], 1)

            def scores(a, n, u, t):
                act.wait_ge(S["shift_ready"], at("shift_ready", a, t + 1))
                nc.scalar.activation(sink_exp[:, t, :], sink_arg[:, t, :], ACT.Exp)
                for i in range(8):
                    ex = nc.scalar.activation(
                        xs[:, t, i * P:(i + 1) * P],
                        ps[:, SCORE_BANK[t] + i // 4, (i % 4) * P:(i % 4 + 1) * P], ACT.Exp,
                        bias=shift[:, t, i:i + 1], accum_out=row_sum[:, t, i:i + 1])
                ex.then_inc(S["exp_done"], 1)

            def spread(a, n, u, t):
                act.wait_ge(S["spread_done"], at("spread_done", a, t + 1))
                bank = SCORE_BANK[t]
                nc.scalar.activation(PT[:].rearrange("p v c q -> p v (c q)"), ps[:, bank:bank + 2, :],
                                     ACT.Copy).then_inc(S["PT_ready"], 1)

            def mix(a, n, u, t):
                act.wait_ge(S["mix_done"], at("mix_done", a, t + 1))
                nc.scalar.activation(hT_hi[:, 0:4, t * P:(t + 1) * P],
                                     ps[:, SCORE_BANK[t], :].rearrange("p (j q) -> p j q", j=4),
                                     ACT.Copy).then_inc(S["aT_hi_done"], 1)

            def out_proj(a, n, u, h):
                for k in range(4):
                    split(n, u, k)

            def up(b, n, u, f0, count):
                with act.Fori(0, count // 2) as j:
                    for i in range(2):
                        f = j * 2 + (f0 + i)
                        bank = UP_BANK[f0] + 2 * i
                        split(n + j * 4, u, 2 * i)
                        split(n + j * 4, u, 2 * i + 1)
                        act.wait_ge(S["g_ready"], at("g_ready", b, f - 1))
                        nc.scalar.activation(ub[:, i, :, 2:2 + T], ps[:, bank:bank + 2, :], ACT.Copy)
                        for s in range(2):
                            col = bass.ds(f + s * FT, 1)
                            cv = nc.scalar.activation(cb[:, i, s, :], ps[:, bank + s, :], ACT.Identity,
                                                      bias=cbias[:, col], scale=cw[2][:, col])
                        cv.then_inc(S["u_copied"], 1)
                        act.wait_ge(S["conv_done"], at("conv_done", b, f + 1))
                        act.wait_ge(S["halo_kept"], at("halo_kept", b, f + 1))
                        nc.scalar.activation(ub[:, i, 0, 2:2 + T], cb[:, i, 0, :], ACT.Tanh, scale=0.5
                                             ).then_inc(S["tanh_done"], 1)

            def down(b, n, u, g, h):
                for k in range(GROUPS[g] // 2):
                    split(n, u, k)

            def store(b, n, u):
                act.wait_ge(S["y_added"], at("y_added", b, 32))
                act.dma_start(out_v[:, bass.ds(b * NT, NT), :], res[:]).then_inc(S["stored"], 16)

            act.sem_inc(S["u_copied"], START["u_copied"])
            for k in range(RING):
                split(0, 0, k - RING)
            act.wait_ge(const_ready, CONST_READY)
            walk(act, stages_of(norm=norm, turn=turn, pool_in=pool_in, q_in=q_in, kv_in=kv_in, heads=heads,
                                scores=scores, spread=spread, mix=mix, out=out_proj, up=up, down=down,
                                store=store))
            act.wait_ge(S["stored"], at("stored", NB - 1, 16))

        @block.vector
        def _(dve):
            v = nc.vector

            def split(n, u, k):
                m, r, s = k + RING, (u + k + RING) % RAW, (u + k + RING) % RING
                if isinstance(n, int) and n + m >= N_ALL:
                    return
                dve.wait_ge(split_hi, n + (m + 1))
                v.tensor_tensor(w_lo[:, s, :], raw[:, r, :], as_f32(w_hi[:, s, :]), ALU.subtract
                                ).then_inc(split_lo, 1)

            def tile_done(name, b, k, n, units, t):
                if t < NT - 1:
                    dve.wait_ge(S[name], at(name, b, k))
                else:
                    dve.wait_ge(unit_used, n + units)

            def turn(a, n, u, i):
                for dt in range(KT):
                    dve.wait_ge(S["hT_hi_done"], at("hT_hi_done", a, 8 * i + dt + 1))
                    v.scalar_tensor_tensor(hT_lo[:, dt, :], ps[:, TURN_BANK[i] + dt % 4, :],
                                           gain[i][:, dt:dt + 1], as_f32(hT_hi[:, dt, :]),
                                           ALU.mult, ALU.subtract).then_inc(S["hT_lo_done"], 1)

            STEP0 = (0, 3, 7, 12)

            def window(a, g):
                dve.wait_ge(S["p_copied"], at("p_copied", a, g + 1))
                step, p_g = STEP0[g], pbuf[:, g % 2, :]
                src, lag = p_g, 1
                for k in range(g + 1):
                    lo = 2 * lag - 1
                    dst = sums[:, k % 2, :]
                    v.tensor_tensor(dst[:, lo:], src[:, lo:], src[:, lo - lag:T + CARRY - lag], ALU.add
                                    ).then_inc(S["win_step"], 1)
                    step += 1
                    dve.wait_ge(S["win_step"], at("win_step", a, step))
                    src, lag = dst, 2 * lag
                if first_block(a):
                    v.tensor_tensor(src[:, CARRY:2 * CARRY], src[:, CARRY:2 * CARRY], ratio[:, g, :], ALU.mult
                                    ).then_inc(const_step, 1)
                    dve.wait_ge(const_step, CONST_STEP + g + 1)
                v.scalar_tensor_tensor(p_g[:, CARRY:], src[:, CARRY:], 1.0 / WINDOWS[g], p_g[:, CARRY:],
                                       ALU.mult, ALU.subtract).then_inc(S["win_step"], 1)
                step += 1
                if g > 0:
                    dve.wait_ge(S["pool_done"], at("pool_done", a, g))
                dve.wait_ge(S["win_step"], at("win_step", a, step))
                v.tensor_copy(mix_hi[:], p_g[:, CARRY:]).then_inc(S["win_step"], 1)

            def window_end(a, g):
                dve.wait_ge(S["win_step"], at("win_step", a, STEP0[g] + g + 3))
                v.tensor_tensor(mix_lo[:], pbuf[:, g % 2, CARRY:], as_f32(mix_hi[:]), ALU.subtract
                                ).then_inc(S["mix_ready"], 1)

            def pool_in(a, n, u):
                split(n, u, 0)
                split(n, u, 1)
                window(a, 0)
                window_end(a, 0)
                split(n, u, 2)
                split(n, u, 3)

            def q_in(a, n, u):
                def summed(t):
                    dve.wait_ge(S["q_squared"], at("q_squared", a, t + 1))
                    v.tensor_reduce(ss_q[:, t, :], xs[:, t, 0:QC].rearrange("p (h d) -> p h d", h=8),
                                    AX.X, ALU.add).then_inc(S["q_summed"], 1)

                def scaled(t):
                    dve.wait_ge(S["q_rstd"], at("q_rstd", a, t + 1))
                    v.tensor_tensor(xs[:, t, 0:QC].rearrange("p (j v d) -> p v j d", v=2, j=4),
                                    ps[:, Q_BANK + t, :].rearrange("p (v j d) -> p v j d", v=2, j=4),
                                    rs_q[:, t, :].rearrange("p (v j) -> p v j", v=2).unsqueeze(3)
                                    .broadcast_to([P, 2, 4, HD]), ALU.mult
                                    ).then_inc(S["q_scaled"], 1)

                split(n, u, 0)
                split(n, u, 1)
                window(a, 1)
                window_end(a, 1)
                split(n, u, 2)
                window(a, 2)
                window_end(a, 2)
                split(n, u, 3)
                summed(0)
                summed(1)
                window(a, 3)
                window_end(a, 3)
                scaled(0)
                summed(2)
                scaled(1)
                summed(3)
                scaled(2)
                scaled(3)

            def kv_in(a, n, u):
                split(n, u, 0)
                split(n, u, 1)

                def scaled(t):
                    dve.wait_ge(S["k_rstd"], at("k_rstd", a, t + 1))
                    v.tensor_tensor(xs[:, t, QC:QC + KVC].rearrange("p (h d) -> p h d", h=2),
                                    ps[:, KV_BANK + t, 0:KVC].rearrange("p (h d) -> p h d", h=2),
                                    rs_k[:, t, :].unsqueeze(2).broadcast_to([P, 2, HD]), ALU.mult
                                    ).then_inc(S["k_scaled"], 1)

                for t in range(NT):
                    dve.wait_ge(S["k_squared"], at("k_squared", a, t + 1))
                    v.tensor_reduce(ss_k[:, t, :], xs[:, t, QC:QC + KVC].rearrange("p (h d) -> p h d", h=2),
                                    AX.X, ALU.add).then_inc(S["k_summed"], 1)
                    if t:
                        scaled(t - 1)
                scaled(NT - 1)
                dve.wait_ge(S["m_copied"], at("m_copied", a, 4))
                dve.wait_ge(unit_used, n + 2)
                for g in range(4):
                    v.tensor_copy(hT_hi[:, 4 + g, :], mf[:, g, :]).then_inc(S["mT_step"], 1)
                for g in range(4):
                    dve.wait_ge(S["mT_step"], at("mT_step", a, g + 1))
                    v.tensor_tensor(hT_lo[:, 4 + g, :], mf[:, g, :], as_f32(hT_hi[:, 4 + g, :]), ALU.subtract
                                    ).then_inc(S["mT_ready"], 1)

            def inverse(a, t):
                dve.wait_ge(S["exp_done"], at("exp_done", a, t + 1))
                v.tensor_tensor(den[:, t, :], row_sum[:, t, :], sink_exp[:, t, :], ALU.add
                                ).then_inc(S["sm_step"], 1)
                dve.wait_ge(S["sm_step"], at("sm_step", a, SM_INV[t]))
                v.reciprocal(inv[:, t, :], den[:, t, :]).then_inc(S["inv_ready"], 1)

            SM_SCORE, SM_INV = (0, 2, 6, 9), (5, 6, 9, 12)

            def scores(a, n, u, t):
                bank = SCORE_BANK[t]
                dve.wait_ge(S["score_done"], at("score_done", a, t + 1))
                if first_block(a) and t == 0:
                    for h in range(2):
                        v.memset(ps[:, bank + h, 0:2 * P].rearrange("p (j c k) -> p j c k", j=2, c=2)[:, :, 1, :],
                                 NEG).then_inc(const_step, 1)
                    dve.wait_ge(const_step, CONST_STEP + 6)
                v.tensor_reduce(mx[:, t, :].rearrange("p (v i) -> p v i", v=2),
                                ps[:, bank:bank + 2, :].rearrange("p v (i k) -> p v i k", i=4),
                                AX.X, ALU.max).then_inc(S["sm_step"], 1)
                dve.wait_ge(S["sm_step"], at("sm_step", a, SM_S[t] + 1))
                v.scalar_tensor_tensor(shift[:, t, :], mx[:, t, :], -1.0, neg_sink[:], ALU.mult, ALU.min
                                       ).then_inc(S["sm_step"], 1)
                dve.wait_ge(S["sm_step"], at("sm_step", a, SM_S[t] + 2))
                v.tensor_tensor(sink_arg[:, t, :], sink[:], shift[:, t, :], ALU.add
                                ).then_inc(S["shift_ready"], 1)
                if t == 1:
                    inverse(a, 0)

            SM_S = (0, 2, 6, 9)

            def spread(a, n, u, t):
                if t + 1 < NT:
                    inverse(a, t + 1)

            def mix(a, n, u, t):
                dve.wait_ge(S["aT_hi_done"], at("aT_hi_done", a, t + 1))
                v.tensor_tensor(hT_lo[:, 0:4, t * P:(t + 1) * P],
                                ps[:, SCORE_BANK[t], :].rearrange("p (j q) -> p j q", j=4),
                                as_f32(hT_hi[:, 0:4, t * P:(t + 1) * P]), ALU.subtract
                                ).then_inc(S["aT_lo_done"], 1)

            def out_proj(a, n, u, h):
                for k in range(4):
                    split(n, u, k)
                for t in range(NT):
                    tile_done("out_done", a, 3 * h + t + 1, n, 4, t)
                    c = slice(h * 512, (h + 1) * 512)
                    v.tensor_tensor(x_a[:, t, c], ps[:, OUT_BANK[h] + t, :], x_a[:, t, c], ALU.add
                                    ).then_inc(S["out_added"], 1)

            def up(b, n, u, f0, count):
                with dve.Fori(0, count // 2) as j:
                    for i in range(2):
                        f = j * 2 + (f0 + i)
                        split(n + j * 4, u, 2 * i)
                        split(n + j * 4, u, 2 * i + 1)
                        dve.wait_ge(S["u_copied"], at("u_copied", b, f + 1))
                        dve.wait_ge(S["halo_in"], at("halo_in", b, f + 1))
                        for tap in (1, 0):
                            for s in range(2):
                                if tap == 0:
                                    dve.wait_ge(S["conv_step"], at("conv_step", b, f * 2 + (s + 1)))
                                st = v.scalar_tensor_tensor(cb[:, i, s, :], ub[:, i, s, tap:tap + T],
                                                            cw[tap][:, bass.ds(f + s * FT, 1)],
                                                            cb[:, i, s, :], ALU.mult, ALU.add)
                                if tap == 1:
                                    st.then_inc(S["conv_step"], 1)
                        st.then_inc(S["conv_done"], 1)
                        gate, value = cb[:, i, 0, :], cb[:, i, 1, :]
                        dve.wait_ge(S["tanh_done"], at("tanh_done", b, f + 1))
                        v.scalar_tensor_tensor(gate, ub[:, i, 0, 2:2 + T], 1.0, gate, ALU.add, ALU.mult
                                               ).then_inc(S["silu_step"], 1)
                        dve.wait_ge(S["silu_step"], at("silu_step", b, f * 3 + 1))
                        v.scalar_tensor_tensor(value, gate, 0.5, value, ALU.mult, ALU.mult
                                               ).then_inc(S["silu_step"], 1)
                        dve.wait_ge(S["silu_step"], at("silu_step", b, f * 3 + 2))
                        g_slot = bass.ds(j * 2 + i, 1)
                        v.tensor_copy(g_hi[:, g_slot, :], value.unsqueeze(1)).then_inc(S["silu_step"], 1)
                        dve.wait_ge(S["silu_step"], at("silu_step", b, f * 3 + 3))
                        v.tensor_tensor(g_lo[:, g_slot, :], value.unsqueeze(1), as_f32(g_hi[:, g_slot, :]),
                                        ALU.subtract).then_inc(S["g_ready"], 1)

            def down(b, n, u, g, h):
                if (g, h) == (0, 0):
                    dve.wait_ge(S["res_copied"], at("res_copied", b, 1))
                units = GROUPS[g] // 2
                for k in range(units):
                    split(n, u, k)
                for t in range(NT):
                    tile_done("down_done", b, 3 * (2 * g + h) + t + 1, n, units, t)
                    c = slice(h * 512, (h + 1) * 512)
                    v.tensor_tensor(res[:, t, c], ps[:, DOWN_BANK[g, h] + t, :], res[:, t, c], ALU.add
                                    ).then_inc(S["y_added"], 1)

            dve.sem_inc(S["g_ready"], START["g_ready"])
            for k in range(RING):
                split(0, 0, k - RING)
            dve.wait_ge(const_in, CONST_IN)
            sink_of = sink_row[:].rearrange("p (v j i) -> p i v j", v=2, j=2)
            for i in range(2):
                half = slice(i * HD, (i + 1) * HD)
                for c in range(2):
                    v.tensor_copy(sink[half, :].rearrange("p (v c j) -> p c v j", v=2, c=2)[:, c],
                                  sink_of[half, i]).then_inc(const_step, 1)
            v.tensor_copy(pw_hi[:], pw_in).then_inc(const_step, 1)
            v.tensor_scalar(gk[:], gk_in[:], HD ** -0.5, None, ALU.mult).then_inc(const_ready, 1)
            dve.wait_ge(const_turned, 1)
            v.tensor_copy(cst[:], ps[:, 0, 0:200]).then_inc(const_step, 1)
            dve.wait_ge(const_step, 6)
            v.tensor_scalar(neg_sink[:], sink[:], -1.0, None, ALU.mult).then_inc(const_ready, 1)
            v.tensor_tensor(pw_lo[:], pw_in, as_f32(pw_hi[:]), ALU.subtract).then_inc(const_ready, 1)
            v.tensor_tensor(pbias[:], pbias_in, pscale, ALU.mult).then_inc(const_ready, 1)
            dve.wait_ge(const_pool, CONST_POOL)
            walk(dve, stages_of(turn=turn, pool_in=pool_in, q_in=q_in, kv_in=kv_in,
                                scores=scores, spread=spread, mix=mix, out=out_proj, up=up, down=down))

        @block.gpsimd
        def _(pool):
            g = nc.gpsimd

            def wait(semaphore, value):
                pool.wait_ge(semaphore, value)
                if not isinstance(value, int):
                    pool.sem_inc(pool_waited, 1)

            def inverse_root(dst, src, count, width, step, k_step, done):
                g.tensor_scalar(dst, src, 1.0 / width, EPS, ALU.mult, ALU.add).then_inc(S[step], 1)
                wait(S[step], k_step)
                g.tensor_tensor(dst, dst, half_neg[:, 0:count], ALU.pow).then_inc(S[done], 1)

            def norm(a, n, u, i):
                for t in range(NT):
                    wait(S["sq_done"], at("sq_done", a, 4 * i + t + 1))
                    inverse_root(rstd[:, t:t + 1], ss[:, t:t + 1], 1, D, "rstd_step",
                                 at("rstd_step", a, 4 * i + t + 1), "rstd_done")
                if i == 0:
                    if not first_block(a):
                        wait(S["mix_done"], at("mix_done", a - 1, 4))
                    g.tensor_copy(v_even[:, 0, :], v_even[:, NT, :]).then_inc(S["v_kept"], 1)

            def q_in(a, n, u):
                for t in range(NT):
                    wait(S["q_summed"], at("q_summed", a, t + 1))
                    inverse_root(rs_q[:, t, :], ss_q[:, t, :], 8, HD, "q_step", at("q_step", a, t + 1), "q_rstd")

            def kv_in(a, n, u):
                for t in range(NT):
                    wait(S["k_summed"], at("k_summed", a, t + 1))
                    inverse_root(rs_k[:, t, :], ss_k[:, t, :], 2, HD, "k_step", at("k_step", a, t + 1), "k_rstd")

            def scale_probs(a, t):
                wait(S["inv_ready"], at("inv_ready", a, t + 1))
                pr = xs[:, t, :].rearrange("p (i k) -> p i k", i=8)
                g.tensor_tensor(pr, pr, inv[:, t, :].unsqueeze(2).broadcast_to([P, 8, P]), ALU.mult
                                ).then_inc(S["p_scaled"], 1)

            def scores(a, n, u, t):
                if t == 1:
                    scale_probs(a, 0)

            def spread(a, n, u, t):
                if t + 1 < NT:
                    scale_probs(a, t + 1)

            def up(b, n, u, f0, count):
                with pool.Fori(0, count // 2) as j:
                    for i in range(2):
                        f = j * 2 + (f0 + i)
                        wait(S["g_ready"], at("g_ready", b, f - 1))
                        g.tensor_copy(ub[:, i, :, 0:2], halo[:, bass.ds(f, 1), :, :].squeeze(1)
                                      ).then_inc(S["halo_in"], 1)
                        wait(S["u_copied"], at("u_copied", b, f + 1))
                        wait(S["halo_in"], at("halo_in", b, f + 1))
                        g.tensor_copy(halo[:, bass.ds(f, 1), :, :].squeeze(1), ub[:, i, :, T:T + 2]
                                      ).then_inc(S["halo_kept"], 1)

            def keep(a, n, u):
                if not first_block(a):
                    wait(S["stored"], at("stored", a - 1, 16))
                wait(S["out_added"], at("out_added", a, 8))
                g.tensor_copy(res[:], x_a[:]).then_inc(S["res_copied"], 1)

            g.memset(ident[:], 0.0).then_inc(const_cleared, 1)
            g.memset(ratio[:], 1.0).then_inc(const_cleared, 1)
            wait(const_cleared, 2)
            g.affine_select(out=ident[:], in_=ident[:], compare_op=ALU.not_equal, fill=1.0, base=0,
                            pattern=[[-1, P]], channel_multiplier=1).then_inc(const_pool, 1)
            for i, w in enumerate(WINDOWS):
                for pos in range(w - 1):
                    ms = g.memset(ratio[:, i, pos:pos + 1], float(w) / (pos + 1))
            ms.then_inc(const_pool, 1)
            g.memset(half_neg[:], -0.5).then_inc(const_pool, 1)
            for ap in (k_keep[:], v_even[:], p_keep[:], halo[:]):
                g.memset(ap, 0.0).then_inc(const_pool, 1)
            wait(const_pool, CONST_POOL)
            walk(pool, stages_of(norm=norm, q_in=q_in, kv_in=kv_in, scores=scores, spread=spread,
                                 up=up, keep=keep))


_INS = ["x", "norm1_g", "w_in", "q_norm_g", "k_norm_g", "attn_sinks", "pool_w", "pool_b", "pool_scale",
        "w_out", "norm2_g", "w_up", "conv_w", "conv_b", "w_down"]
_OUTS = [((1, SEQ, D), "float32")]


def kernel(**inputs):
    import numpy as _np
    import concourse.bacc as _bacc
    from concourse import mybir as _mybir
    from concourse.bass_utils import run_bass_kernel_spmd as _run

    nc = _bacc.Bacc("TRN2", target_bir_lowering=False, num_devices=1)
    arrays, args = {}, []
    for name in _INS:
        a = _np.ascontiguousarray(inputs[name])
        arrays[f"in_{name}_dram"] = a
        args.append(nc.dram_tensor(f"in_{name}_dram", a.shape, _mybir.dt.from_np(a.dtype), kind="ExternalInput").ap())
    for i, (shape, dtype) in enumerate(_OUTS):
        dt = _mybir.dt.from_np(_np.dtype(dtype))
        args.append(nc.dram_tensor(f"out_{i}_dram", shape, dt, kind="ExternalOutput").ap())
    bass_hybrid_block(nc, *args)
    r = _run(nc, [arrays], core_ids=[0])
    got = tuple(r.results[0][f"out_{i}_dram"] for i in range(len(_OUTS)))
    return got[0]
```

```python
from contextlib import ExitStack

import concourse.bass as bass
from concourse import mybir

ALU = mybir.AluOpType
ACT = mybir.ActivationFunctionType
AX = mybir.AxisListType
F32 = mybir.dt.float32
F32R = mybir.dt.float32r

P = 128
T = 512
NT = T // P
D = 1024
KT = D // P
SEQ = 2048
NB = SEQ // T
HD = 64
QC = 512
KVC = 128
FF = 2816
FT = FF // P
WINDOWS = (2, 4, 8, 16)
CARRY = 16
EPS = 1e-6
NEG = -1e30

UNIT = 1024
RAW = 2
MIX = 2
RING = 4
GROUPS = (8, 6, 4, 4)
BASE = (0, 8, 14, 18)

ITERATION = [
    ("F", "up", (0, 8), 16), ("F", "down", (0, 0, 0, 4), 4), ("F", "down", (0, 1, 0, 4), 4),
    ("F", "up", (8, 6), 12), ("F", "down", (1, 0, 0, 1), 1), ("A", "norm", (0, 0), 0),
    ("F", "down", (1, 0, 1, 2), 1), ("A", "norm", (0, 1), 0),
    ("F", "down", (1, 0, 2, 3), 1), ("A", "norm", (0, 2), 0),
    ("F", "down", (1, 1, 0, 1), 1), ("A", "norm", (0, 3), 0), ("F", "down", (1, 1, 1, 3), 2),
    ("F", "up", (14, 8), 16), ("F", "down", (2, 0, 0, 2), 2),
    ("A", "turn", (0,), 0), ("A", "pool_in", (), 4), ("A", "q_in", (), 4), ("A", "kv_in", (), 2),
    ("A", "q_turn", (), 0), ("F", "down", (2, 1, 0, 1), 1), ("A", "k_turn", (), 0), ("F", "down", (2, 1, 1, 2), 1),
    ("A", "scores", (0,), 0), ("A", "scores", (1,), 0), ("F", "down", (3, 0, 0, 2), 2),
    ("A", "spread", (0,), 0), ("A", "spread", (1,), 0), ("A", "scores", (2,), 0), ("A", "scores", (3,), 0),
    ("A", "mix", (0,), 0), ("A", "mix", (1,), 0), ("A", "out", (0, 0, 1), 1),
    ("A", "spread", (2,), 0), ("A", "spread", (3,), 0), ("A", "out", (0, 1, 2), 1),
    ("A", "mix", (2,), 0), ("A", "mix", (3,), 0), ("A", "out", (0, 2, 4), 2), ("A", "out", (1, 0, 4), 4),
    ("A", "norm", (1,), 0), ("F", "down", (3, 1, 0, 2), 2), ("A", "turn", (1,), 0),
    ("F", "store", (), 0), ("A", "keep", (), 0),
]
PROLOGUE = [s for s in ITERATION if s[0] == "A"]
EPILOGUE = [s for s in ITERATION if s[0] == "F"]
N_PRO = sum(s[3] for s in PROLOGUE)
N_ITER = sum(s[3] for s in ITERATION)
N_ALL = N_PRO + (NB - 1) * N_ITER + sum(s[3] for s in EPILOGUE)
assert N_ITER % RING == 0 and N_ITER % RAW == 0

UP_BANK = {0: 0, 8: 4, 14: 4}
DOWN_BANK = {(0, 0): 4, (0, 1): 0, (1, 0): 0, (1, 1): 0, (2, 0): 0, (2, 1): 0, (3, 0): 0, (3, 1): 4}
TURN_BANK = ((4, 0), (0, 4))
POOL_BANK, Q_BANK, KV_BANK, Q_TURN_BANK, K_TURN_BANK = 4, 0, 4, 0, 6
SCORE_BANK = (4, 6, 0, 2)
OUT_BANK = (4, 0)

PER = dict(
    sq_done=8, rstd_step=8, rstd_done=8, xs_ready=8, turned=16, hT_hi_done=16, hT_lo_done=16,
    p_carried=4, p_copied=4, win_step=18, mix_ready=4, pool_done=4, m_copied=4, mT_step=4, mT_ready=4,
    q_done=3, q_squared=4, q_summed=4, q_step=4, q_rstd=4, q_scaled=4,
    kv_done=1, k_squared=2, k_summed=2, k_step=2, k_rstd=2, k_scaled=2, v_kept=1,
    kT_done=1, k_placed=1, kT_ready=1, qT_done=4, qT_ready=4,
    score_done=4, sm_step=12, shift_ready=4, exp_done=4, inv_ready=4, p_scaled=4,
    spread_done=4, PT_ready=4, mix_done=4, aT_hi_done=4, aT_lo_done=4,
    out_done=6, out_added=8, res_copied=1,
    u_copied=FT, halo_in=FT, halo_kept=FT, conv_step=2 * FT, conv_done=FT, tanh_done=FT, silu_step=3 * FT,
    g_ready=FT, down_done=24, y_added=32, stored=16 * NT,
)
START = dict(u_copied=2, g_ready=2)


def at(name, block, k):
    return block * PER[name] + (k + START.get(name, 0))


def bass_hybrid_block(nc, x, norm1_g, w_in, q_norm_g, k_norm_g, attn_sinks, pool_w, pool_b, pool_scale,
                      w_out, norm2_g, w_up, conv_w, conv_b, w_down, out):
    x_v = x[0].rearrange("(t p) d -> p t d", p=P)
    out_v = out[0].rearrange("(t p) d -> p t d", p=P)
    w_in_v = w_in[0].rearrange("(k p) n -> p k n", p=P)
    w_out_v = w_out[0].rearrange("(k p) n -> p k n", p=P)
    w_up_v = w_up[0].rearrange("(k p) n -> p k n", p=P)
    w_down_v = w_down[0].rearrange("(k p) n -> p k n", p=P)

    with ExitStack() as ctx:
        def sb(name, shape, dt=F32):
            return ctx.enter_context(nc.sbuf_tensor(name, shape, dt))

        def sem(name):
            return ctx.enter_context(nc.semaphore(name))

        raw = sb("raw", [P, RAW, UNIT])
        w_hi = sb("w_hi", [P, RING, UNIT], F32R)
        w_lo = sb("w_lo", [P, RING, UNIT], F32R)
        x_a = sb("x_a", [P, NT, D])
        res = sb("res", [P, NT, D])
        xs = sb("xs", [P, NT, D])
        hT_hi = sb("hT_hi", [P, KT, T], F32R)
        hT_lo = sb("hT_lo", [P, KT, T], F32R)
        g_hi = sb("g_hi", [P, 8, T], F32R)
        g_lo = sb("g_lo", [P, 8, T], F32R)
        qT = sb("qT", [P, NT, T])
        PT = sb("PT", [P, 2, 2, 4, P])
        kT = sb("kT", [P, NT, 2, 2, HD])
        k_keep = sb("k_keep", [P, HD])
        v_odd = sb("v_odd", [P, NT, KVC])
        v_even = sb("v_even", [P, NT + 1, KVC])
        mix_hi = sb("mix_hi", [P, MIX, T], F32R)
        mix_lo = sb("mix_lo", [P, MIX, T], F32R)
        pw_hi = sb("pw_hi", [P, 4, P], F32R)
        pw_lo = sb("pw_lo", [P, 4, P], F32R)
        work = sb("work", [P, 4104])
        ub = work[:, 0:2056].rearrange("p (r s t) -> p r s t", r=2, s=2)
        cb = work[:, 2056:4104].rearrange("p (r s t) -> p r s t", r=2, s=2)
        pbuf = work[:, 0:4 * (T + CARRY)].rearrange("p (g t) -> p g t", g=4)
        mf = pbuf[:, :, CARRY:]
        sums = work[:, 4 * (T + CARRY):6 * (T + CARRY)].rearrange("p (r t) -> p r t", r=2)
        p_keep = sb("p_keep", [P, 4, CARRY])
        halo = sb("halo", [P, FT, 2, 2])
        cst = sb("cst", [P, 200])
        cw = [cst[:, 0:44], cst[:, 44:88], cst[:, 112:156]]
        cbias = cst[:, 156:200]
        gain = [cst[:, 88:96], cst[:, 96:104]]
        pbias_in, pscale = cst[:, 104:108], cst[:, 108:112]
        pbias = sb("pbias", [P, 4])
        gq = sb("gq", [P, 1])
        gk_in = sb("gk_in", [P, 1])
        gk = sb("gk", [P, 1])
        sink_row = sb("sink_row", [P, 8])
        sink = sb("sink", [P, 8])
        neg_sink = sb("neg_sink", [P, 8])
        half_neg = sb("half_neg", [P, 8])
        ident = sb("ident", [P, P])
        ss = sb("ss", [P, NT])
        rstd = sb("rstd", [P, NT])
        ss_q = sb("ss_q", [P, NT, 8])
        rs_q = ss_q
        ss_k = sb("ss_k", [P, NT, 2])
        rs_k = sb("rs_k", [P, NT, 2])
        mx = sb("mx", [P, NT, 8])
        shift = sb("shift", [P, NT, 8])
        sink_exp = sb("sink_exp", [P, NT, 8])
        row_sum = sb("row_sum", [P, NT, 8])
        ps = ctx.enter_context(nc.psum_tensor("ps", [P, 8, 512], F32))

        S = {name: sem(name) for name in PER}
        x_loaded = [sem(f"x_loaded{t}") for t in range(NT)]
        raw_in = [sem(f"raw_in{i}") for i in range(RAW)]
        split_hi, split_lo, unit_used = sem("split_hi"), sem("split_lo"), sem("unit_used")
        const_in, const_pool, const_cleared = sem("const_in"), sem("const_pool"), sem("const_cleared")
        sp_waited, pe_waited, pool_waited = sem("sp_waited"), sem("pe_waited"), sem("pool_waited")
        const_turned, const_step, const_ready = sem("const_turned"), sem("const_step"), sem("const_ready")

        ratio = res[:, 2, 0:4 * CARRY].rearrange("p (g t) -> p g t", g=4)
        vec_rows = res[:, 0, 0:256].rearrange("p (a n) -> p a n", a=2)
        pw_in = res[:, 1, 0:512].rearrange("p (g n) -> p g n", g=4)

        def as_f32(ap):
            return ap.bitcast(F32)

        def walk(engine, stages):
            def run(order, block_f, block_a, n, u):
                for side, name, args, units in order:
                    stages[name](block_a if side == "A" else block_f, n, u, *args)
                    n, u = n + units, u + units
            run(PROLOGUE, None, 0, 0, 0)
            with engine.Fori(0, NB - 1) as it:
                run(ITERATION, it, it + 1, it * N_ITER + N_PRO, N_PRO)
            run(EPILOGUE, NB - 1, None, N_PRO + (NB - 1) * N_ITER, N_PRO)

        def last_block(b):
            return isinstance(b, int) and b == NB - 1

        def first_block(a):
            return isinstance(a, int) and a == 0

        def stages_of(**have):
            names = {s[1] for s in ITERATION}
            return {name: have.get(name, lambda *_: None) for name in names}

        CONST_IN = 14 * 16
        CONST_POOL = 7
        CONST_STEP, CONST_READY = 6, 4

        block = ctx.enter_context(nc.Block())

        @block.sync
        def _(sp):
            def load(n, u, k, src):
                r = (u + k) % RAW
                if not isinstance(n, int) or n + k >= RAW:
                    sp.wait_ge(split_lo, n + (k - RAW + 1))
                    if not isinstance(n, int):
                        sp.sem_inc(sp_waited, 1)
                sp.dma_start(raw[:, r, :].rearrange("p (k n) -> p k n", k=src.shape[1]), src).then_inc(raw_in[r], 16)

            def load_x(a):
                if not first_block(a):
                    sp.wait_ge(S["xs_ready"], at("xs_ready", a - 1, 8))
                    sp.sem_inc(sp_waited, 1)
                    sp.wait_ge(S["res_copied"], at("res_copied", a - 1, 1))
                    sp.sem_inc(sp_waited, 1)
                for t in range(NT):
                    tile = slice(a * NT + t, a * NT + t + 1) if isinstance(a, int) else bass.ds(a * NT + t, 1)
                    sp.dma_start(x_a[:, t:t + 1, :], x_v[:, tile, :]).then_inc(x_loaded[t], 16)

            def up(b, n, u, f0, count):
                with sp.Fori(0, count // 2) as j:
                    for i in range(4):
                        col = j * (2 * P) + ((f0 + i // 2) * P + (i % 2) * FF)
                        load(j * 4 + n, u, i, w_up_v[:, :, bass.ds(col, P)])
                if f0 == 0 and not last_block(b):
                    load_x(b + 1)

            def down(b, n, u, g, h, k0, k1):
                for k in range(k0, k1):
                    kt = BASE[g] + 2 * k
                    load(n, u, k - k0, w_down_v[:, kt:kt + 2, h * 512:(h + 1) * 512])

            def pool_in(a, n, u):
                for g in range(4):
                    c = QC + 2 * KVC + g * P
                    load(n, u, g, w_in_v[:, :, c:c + P])

            def q_in(a, n, u):
                for k in range(4):
                    load(n, u, k, w_in_v[:, 2 * k:2 * k + 2, 0:QC])

            def kv_in(a, n, u):
                for k in range(2):
                    load(n, u, k, w_in_v[:, 4 * k:4 * k + 4, QC:QC + 2 * KVC])

            def out_proj(a, n, u, h, k0, k1):
                for k in range(k0, k1):
                    kt = (4 + 2 * k) % KT
                    load(n, u, k - k0, w_out_v[:, kt:kt + 2, h * 512:(h + 1) * 512])

            load_x(0)
            for row, a, src in [(0, 0, conv_w[0, 0]), (44, 0, conv_w[0, 1]), (88, 0, norm1_g[0]),
                                (96, 0, norm2_g[0]), (104, 0, pool_b[0].rearrange("a b -> (a b)")),
                                (108, 0, pool_scale[0]), (0, 1, conv_w[0, 2]), (44, 1, conv_b[0])]:
                v = src.rearrange("(f p) -> f p", p=P)
                sp.dma_start(vec_rows[row:row + v.shape[0], a, :], v).then_inc(const_in, 16)
            sp.dma_start(pw_in, pool_w[0].rearrange("g c d -> c g d")).then_inc(const_in, 16)
            for i in range(2):
                half = slice(i * HD, (i + 1) * HD)
                sp.dma_start(gq[half, :], q_norm_g.rearrange("o d -> d o")).then_inc(const_in, 16)
                sp.dma_start(gk_in[half, :], k_norm_g.rearrange("o d -> d o")).then_inc(const_in, 16)
            sp.dma_start(sink_row[:], attn_sinks[0:1, :].broadcast_to([P, 8])).then_inc(const_in, 16)
            walk(sp, stages_of(up=up, down=down, pool_in=pool_in, q_in=q_in, kv_in=kv_in, out=out_proj))

        @block.tensor
        def _(pe):
            def passes(out_ap, l_hi, l_lo, r_hi, r_lo, first, last):
                pe.matmul(out_ap, l_hi, r_hi, start=first, stop=False)
                pe.matmul(out_ap, l_hi, r_lo, start=False, stop=False)
                return pe.matmul(out_ap, l_lo, r_hi, start=False, stop=last)

            def by_token(n, u, k0, k1, units, per_unit, place, left, signal, tile_wait, unit_wait=None,
                         tiles_of_bank=1):
                for k in range(k0, k1):
                    if unit_wait:
                        unit_wait(k)
                    pe.wait_ge(split_lo, n + (k - k0 + 1))
                    s = (u + k - k0) % RING
                    hi = w_hi[:, s, :].rearrange("p (k n) -> p k n", k=per_unit)
                    lo = w_lo[:, s, :].rearrange("p (k n) -> p k n", k=per_unit)
                    done = k == units - 1
                    steps = [(kk, t) for kk in range(per_unit) for t in range(NT)]
                    if done or k == 2:
                        steps = [(kk, t) for t in range(NT) for kk in range(per_unit)]
                    for kk, t in steps:
                        i = k * per_unit + kk
                        if kk == 0:
                            tile_wait(k, t)
                        l_hi, l_lo = left(i, t)
                        mm = passes(place(t), l_hi, l_lo, hi[:, kk, :], lo[:, kk, :],
                                    i == 0 and t % tiles_of_bank == 0,
                                    i == per_unit * units - 1 and (t + 1) % tiles_of_bank == 0)
                        if done and kk == per_unit - 1 and t < NT - 1 and (t + 1) % tiles_of_bank == 0:
                            mm.then_inc(S[signal], 1)
                    mm.then_inc(unit_used, 1)

            def tokens(t):
                return slice(t * P, (t + 1) * P)

            def up(b, n, u, f0, count):
                if f0 == 8:
                    pe.wait_ge(S["y_added"], at("y_added", b, 4))
                    if not isinstance(b, int):
                        pe.sem_inc(pe_waited, 1)
                with pe.Fori(0, count // 2) as j:
                    for i in range(2):
                        bank = UP_BANK[f0] + 2 * i
                        pe.wait_ge(S["u_copied"], at("u_copied", b, j * 2 + (f0 + i - 1)))
                        for s in range(2):
                            pe.wait_ge(split_lo, n + (j * 4 + (2 * i + s + 1)))
                            w = (u + 2 * i + s) % RING
                            for k in range(KT):
                                if f0 == 0 and i == 0 and s == 0:
                                    pe.wait_ge(S["hT_lo_done"], at("hT_lo_done", b, 8 + k + 1))
                                c = slice(k * P, (k + 1) * P)
                                mm = passes(ps[:, bank + s, :], w_hi[:, w, c], w_lo[:, w, c],
                                            hT_hi[:, k, :], hT_lo[:, k, :], k == 0, k == KT - 1)
                            mm.then_inc(unit_used, 1)

            def down(b, n, u, g, h, k0, k1):
                def added(g, h, t):
                    return S["y_added"], at("y_added", b, 4 * (2 * g + h) + t + 1)

                def tile_wait(k, t):
                    if k > 0:
                        return
                    if (g, h) == (0, 1):
                        pe.wait_ge(S["u_copied"], at("u_copied", b, 8))
                    elif (g, h) in ((1, 0), (1, 1), (2, 0)):
                        pe.wait_ge(*added(*{(1, 0): (0, 1), (1, 1): (1, 0), (2, 0): (1, 1)}[g, h], t))
                    elif (g, h) == (2, 1) and not last_block(b):
                        pe.wait_ge(S["qT_ready"], at("qT_ready", b + 1, t + 1))
                    elif (g, h) == (2, 1):
                        pe.wait_ge(*added(2, 0, t))
                    elif (g, h) == (3, 0):
                        pe.wait_ge(*added(2, 1, t))
                    elif (g, h) == (3, 1) and not last_block(b):
                        pe.wait_ge(S["out_added"], at("out_added", b + 1, t + 1))
                    elif (g, h) == (3, 1):
                        pe.wait_ge(S["u_copied"], at("u_copied", b, FT))

                slot0 = {0: 0, 1: 0, 2: 0, 3: 4}[g]
                by_token(n, u, k0, k1, GROUPS[g] // 2, 2, lambda t: ps[:, DOWN_BANK[g, h] + t, :],
                         lambda i, t: (g_hi[:, slot0 + i, tokens(t)], g_lo[:, slot0 + i, tokens(t)]),
                         "down_done", tile_wait,
                         lambda k: pe.wait_ge(S["g_ready"], at("g_ready", b, BASE[g] + 2 * k + 2)))

            def turn(a, n, u, i):
                for dt in range(KT):
                    bank = TURN_BANK[i][dt // 4] + dt % 4
                    if i == 0 and first_block(a):
                        pe.wait_ge(const_ready, CONST_READY)
                    elif i == 0 and dt < 4:
                        pe.wait_ge(S["u_copied"], at("u_copied", a - 1, FT))
                    elif i == 0:
                        pe.wait_ge(S["y_added"], at("y_added", a - 1, 16 + dt - 3))
                    elif dt < 4:
                        pe.wait_ge(S["out_added"], at("out_added", a, 4 + dt + 1))
                    elif not first_block(a):
                        pe.wait_ge(S["y_added"], at("y_added", a - 1, 28 + dt - 3))
                    else:
                        pe.wait_ge(S["out_added"], at("out_added", a, dt - 3))
                    if dt == 0:
                        pe.wait_ge(S["xs_ready"], at("xs_ready", a, 4 * i + 4))
                    for t in range(NT):
                        mm = pe.transpose(ps[:, bank, tokens(t)], xs[:, t, dt * P:(dt + 1) * P], ident[:])
                    mm.then_inc(S["turned"], 1)

            def pool_in(a, n, u):
                for g in range(4):
                    pe.wait_ge(split_lo, n + (g + 1))
                    w = (u + g) % RING
                    for k in range(KT):
                        if g == 0:
                            pe.wait_ge(S["hT_lo_done"], at("hT_lo_done", a, k + 1))
                        c = slice(k * P, (k + 1) * P)
                        mm = passes(ps[:, POOL_BANK + g, :], w_hi[:, w, c], w_lo[:, w, c],
                                    hT_hi[:, k, :], hT_lo[:, k, :], k == 0, k == KT - 1)
                    mm.then_inc(unit_used, 1)

            def h_left(i, t):
                return hT_hi[:, i, tokens(t)], hT_lo[:, i, tokens(t)]

            def q_in(a, n, u):
                def pool_map(g):
                    pe.wait_ge(S["mix_ready"], at("mix_ready", a, g + 1))
                    pe.wait_ge(S["p_copied"], at("p_copied", a, g + 1))
                    passes(ps[:, POOL_BANK + g, :], pw_hi[:, g, :], pw_lo[:, g, :],
                           mix_hi[:, g % MIX, :], mix_lo[:, g % MIX, :], True, True).then_inc(S["pool_done"], 1)

                by_token(n, u, 0, 4, 4, 2, lambda t: ps[:, Q_BANK + t, :], h_left, "q_done",
                         lambda k, t: None, pool_map)

            def kv_in(a, n, u):
                by_token(n, u, 0, 2, 2, 4,
                         lambda t: ps[:, KV_BANK + t // 2, (t % 2) * 2 * KVC:(t % 2 + 1) * 2 * KVC],
                         h_left, "kv_done",
                         lambda k, t: pe.wait_ge(S["m_copied"], at("m_copied", a, t // 2 + 1))
                         if k == 0 and t % 2 == 0 else None, tiles_of_bank=2)

            def q_turn(a, n, u):
                for t in range(NT):
                    pe.wait_ge(S["q_scaled"], at("q_scaled", a, t + 1))
                    for j in range(4):
                        q_t = ps[:, Q_TURN_BANK + t, :].rearrange("p (c j q) -> p j c q", c=2, j=4)[:, j]
                        mm = pe.transpose(q_t, xs[:, t, j * P:(j + 1) * P], ident[:])
                    mm.then_inc(S["qT_done"], 1)

            def k_turn(a, n, u):
                pe.wait_ge(S["m_copied"], at("m_copied", a, 3))
                pe.wait_ge(S["k_scaled"], at("k_scaled", a, 2))
                for t in range(NT):
                    mm = pe.transpose(ps[:, K_TURN_BANK, tokens(t)], xs[:, t, QC:QC + KVC], ident[:])
                mm.then_inc(S["kT_done"], 1)

            def scores(a, n, u, t):
                if t == 0:
                    pe.wait_ge(S["qT_ready"], at("qT_ready", a, 4))
                    pe.wait_ge(S["kT_ready"], at("kT_ready", a, 1))
                if t >= 2 and not first_block(a):
                    pe.wait_ge(S["y_added"], at("y_added", a - 1, 24 + 2 * (t - 1)))
                for v in range(2):
                    rows = slice(v * HD, (v + 1) * HD)
                    for c in range(2):
                        for j in range(2):
                            q = slice((2 * c + j) * P, (2 * c + j + 1) * P)
                            mm = pe.matmul(ps[:, SCORE_BANK[t] + v, q], qT[rows, t, q],
                                           kT[rows, t, c].rearrange("p a d -> p (a d)"), start=True, stop=True)
                mm.then_inc(S["score_done"], 1)

            def spread(a, n, u, t):
                pe.wait_ge(S["p_scaled"], at("p_scaled", a, t + 1))
                for i in range(8):
                    mm = pe.transpose(ps[:, SCORE_BANK[t] + i // 4, (i % 4) * P:(i % 4 + 1) * P],
                                      xs[:, t, i * P:(i + 1) * P], ident[:])
                mm.then_inc(S["spread_done"], 1)

            def mix(a, n, u, t):
                pe.wait_ge(S["PT_ready"], at("PT_ready", a, t + 1))
                for v in range(2):
                    d = slice(v * HD, (v + 1) * HD)
                    for c, window in enumerate((v_even, v_odd)):
                        for i in range(2):
                            q = slice(i * HD, (i + 1) * HD)
                            o = ps[q, SCORE_BANK[t], v * 256:(v + 1) * 256] \
                                .rearrange("p (j c q) -> p c j q", j=2, c=2)[:, c]
                            mm = pe.matmul(o, window[:, t, d], PT[:, t % 2, v, 2 * c:2 * c + 2, q],
                                           start=True, stop=True)
                mm.then_inc(S["mix_done"], 1)

            def out_proj(a, n, u, h, k0, k1):
                def left(i, t):
                    return h_left((4 + i) % KT, t)

                def tile_wait(k, t):
                    if h == 0 and k == 0 and t % 2 == 0:
                        pe.wait_ge(S["aT_lo_done"], at("aT_lo_done", a, 1 + t // 2))
                    if h == 0 and k == 2:
                        pe.wait_ge(S["aT_lo_done"], at("aT_lo_done", a, t + 1))

                def unit_wait(k):
                    if h == 0 and k < 2:
                        pe.wait_ge(S["mT_ready"], at("mT_ready", a, 2 * k + 2))
                by_token(n, u, k0, k1, 4, 2, lambda t: ps[:, OUT_BANK[h] + t, :], left, "out_done",
                         tile_wait, unit_wait)

            pe.wait_ge(const_pool, CONST_POOL)
            pe.wait_ge(const_in, CONST_IN)
            pe.transpose(ps[:, 0, 0:112], vec_rows[0:112, 0, :], ident[0:112, 0:112])
            pe.transpose(ps[:, 0, 112:200], vec_rows[0:88, 1, :], ident[0:88, 0:88]).then_inc(const_turned, 1)
            walk(pe, stages_of(up=up, down=down, turn=turn, pool_in=pool_in, q_in=q_in, kv_in=kv_in,
                               q_turn=q_turn, k_turn=k_turn, scores=scores, spread=spread, mix=mix, out=out_proj))

        @block.scalar
        def _(act):
            def split(n, u, k):
                m, r, s = k + RING, (u + k + RING) % RAW, (u + k + RING) % RING
                if isinstance(n, int) and n + m >= N_ALL:
                    return
                if not isinstance(n, int) or n + k >= 0:
                    act.wait_ge(unit_used, n + (k + 1))
                act.wait_ge(raw_in[r], (n + m) * (16 // RAW) + (16 - r * (16 // RAW)))
                nc.scalar.activation(w_hi[:, s, :], raw[:, r, :], ACT.Copy).then_inc(split_hi, 1)

            def tile_done(name, b, k, n, units, t):
                if t < NT - 1:
                    act.wait_ge(S[name], at(name, b, k))
                else:
                    act.wait_ge(unit_used, n + units)

            def norm(a, n, u, i, only=None):
                def square(t):
                    if i == 1:
                        act.wait_ge(S["out_added"], at("out_added", a, 4 + t + 1))
                    else:
                        act.wait_ge(x_loaded[t], a * 16 + 16)
                    nc.scalar.activation(xs[:, t, :], x_a[:, t, :], ACT.Square,
                                         accum_out=ss[:, t:t + 1]).then_inc(S["sq_done"], 1)

                def scale(t):
                    act.wait_ge(S["rstd_done"], at("rstd_done", a, 4 * i + t + 1))
                    nc.scalar.activation(xs[:, t, :], x_a[:, t, :], ACT.Copy,
                                         scale=rstd[:, t:t + 1]).then_inc(S["xs_ready"], 1)

                if i == 0 and only == 0 and not first_block(a):
                    act.wait_ge(S["spread_done"], at("spread_done", a - 1, 4))
                if only is not None:
                    square(only)
                    scale(only)
                    return
                for t in range(NT):
                    square(t)
                    if t:
                        scale(t - 1)
                scale(NT - 1)

            def turn(a, n, u, i):
                for dt in range(KT):
                    act.wait_ge(S["turned"], at("turned", a, 8 * i + dt + 1))
                    nc.scalar.activation(hT_hi[:, dt, :], ps[:, TURN_BANK[i][dt // 4] + dt % 4, :], ACT.Copy,
                                         scale=gain[i][:, dt:dt + 1]).then_inc(S["hT_hi_done"], 1)

            def pool_in(a, n, u):
                if not first_block(a):
                    act.wait_ge(S["g_ready"], at("g_ready", a - 1, FT))
                    act.wait_ge(S["halo_kept"], at("halo_kept", a - 1, FT))
                for g in range(4):
                    split(n, u, g)
                    pool_copy(a, n, g)

            def pool_copy(a, n, g):
                act.wait_ge(unit_used, n + (g + 1))
                buf, bank = pbuf[:, g, :], ps[:, POOL_BANK + g, :]
                nc.scalar.activation(buf[:, 0:CARRY], p_keep[:, g, :], ACT.Copy).then_inc(S["p_carried"], 1)
                nc.scalar.activation(buf[:, CARRY:], bank, ACT.Copy)
                act.wait_ge(S["p_carried"], at("p_carried", a, g + 1))
                nc.scalar.activation(p_keep[:, g, :], bank[:, T - CARRY:T], ACT.Copy).then_inc(S["p_copied"], 1)

            def q_in(a, n, u):
                def pooled(g):
                    act.wait_ge(S["pool_done"], at("pool_done", a, g + 1))
                    nc.scalar.activation(mf[:, g, :], ps[:, POOL_BANK + g, :], ACT.Identity,
                                         bias=pbias[:, g:g + 1], scale=pscale[:, g:g + 1]
                                         ).then_inc(S["m_copied"], 1)

                def square(t):
                    tile_done("q_done", a, t + 1, n, 4, t)
                    nc.scalar.activation(xs[:, t, 0:QC], ps[:, Q_BANK + t, :], ACT.Square
                                         ).then_inc(S["q_squared"], 1)

                for k in range(4):
                    split(n, u, k)
                    pooled(k)
                for t in range(NT):
                    square(t)

            def kv_in(a, n, u):
                split(n, u, 0)
                split(n, u, 1)
                act.wait_ge(S["v_kept"], at("v_kept", a, 1))
                for r in range(2):
                    if r == 0:
                        act.wait_ge(S["kv_done"], at("kv_done", a, 1))
                    else:
                        act.wait_ge(unit_used, n + 2)
                    kv = ps[:, KV_BANK + r, :].rearrange("p (t s n) -> p t s n", t=2, s=2)
                    k_in, v_in, t = kv[:, :, 0, :], kv[:, :, 1, :], 2 * r
                    nc.scalar.activation(v_odd[:, t:t + 2, :], v_in, ACT.Copy)
                    nc.scalar.activation(v_even[0:HD, t:t + 2, :], v_in[0:HD], ACT.Copy)
                    nc.scalar.activation(v_even[HD:P, t + 1:t + 3, :], v_in[HD:P], ACT.Copy)
                    nc.scalar.activation(xs[:, t:t + 2, QC:QC + KVC], k_in, ACT.Square
                                         ).then_inc(S["k_squared"], 1)

            def k_turn(a, n, u):
                act.wait_ge(S["kT_done"], at("kT_done", a, 1))
                nc.scalar.activation(kT[:, 0, 0, 1], k_keep[:], ACT.Copy).then_inc(S["k_placed"], 1)
                by_chunk = ps[:, K_TURN_BANK, :].rearrange("p (t c d) -> p t c d", t=NT, c=2)
                even, odd = by_chunk[:, :, 0, :], by_chunk[:, :, 1, :]
                for dst, src in [(kT[:, :, 0, 0], even), (kT[:, :, 1, 0], even), (kT[:, :, 1, 1], odd),
                                 (kT[:, 1:NT, 0, 1], odd[:, 0:NT - 1])]:
                    nc.scalar.activation(dst, src, ACT.Copy, scale=gk[:, 0:1])
                act.wait_ge(S["k_placed"], at("k_placed", a, 1))
                nc.scalar.activation(k_keep[:], odd[:, NT - 1], ACT.Copy, scale=gk[:, 0:1]
                                     ).then_inc(S["kT_ready"], 1)

            def q_turn(a, n, u):
                for t in range(NT):
                    act.wait_ge(S["qT_done"], at("qT_done", a, t + 1))
                    nc.scalar.activation(qT[:, t, :], ps[:, Q_TURN_BANK + t, :], ACT.Copy,
                                         scale=gq[:, 0:1]).then_inc(S["qT_ready"], 1)

            def exps(a, t):
                act.wait_ge(S["shift_ready"], at("shift_ready", a, t + 1))
                nc.scalar.activation(sink_exp[:, t, :], sink_exp[:, t, :], ACT.Exp)
                for i in range(8):
                    ex = nc.scalar.activation(
                        xs[:, t, i * P:(i + 1) * P],
                        ps[:, SCORE_BANK[t] + i // 4, (i % 4) * P:(i % 4 + 1) * P], ACT.Exp,
                        bias=shift[:, t, i:i + 1], accum_out=row_sum[:, t, i:i + 1])
                ex.then_inc(S["exp_done"], 1)

            def scores(a, n, u, t):
                if t < 3:
                    exps(a, t)

            def spread(a, n, u, t):
                act.wait_ge(S["spread_done"], at("spread_done", a, t + 1))
                if t >= 2:
                    act.wait_ge(S["mix_done"], at("mix_done", a, t - 1))
                bank = SCORE_BANK[t]
                nc.scalar.activation(PT[:, t % 2].rearrange("p v c q -> p v (c q)"), ps[:, bank:bank + 2, :],
                                     ACT.Copy).then_inc(S["PT_ready"], 1)

            def mix(a, n, u, t):
                act.wait_ge(S["mix_done"], at("mix_done", a, t + 1))
                nc.scalar.activation(hT_hi[:, 0:4, t * P:(t + 1) * P],
                                     ps[:, SCORE_BANK[t], :].rearrange("p (j q) -> p j q", j=4),
                                     ACT.Copy).then_inc(S["aT_hi_done"], 1)
                if t == 1:
                    exps(a, 3)

            def out_proj(a, n, u, h, k0, k1):
                for k in range(k1 - k0):
                    split(n, u, k)

            def up(b, n, u, f0, count):
                with act.Fori(0, count // 2) as j:
                    for i in range(2):
                        f = j * 2 + (f0 + i)
                        bank = UP_BANK[f0] + 2 * i
                        split(n + j * 4, u, 2 * i)
                        split(n + j * 4, u, 2 * i + 1)
                        act.wait_ge(S["g_ready"], at("g_ready", b, f - 1))
                        nc.scalar.activation(ub[:, i, :, 2:2 + T], ps[:, bank:bank + 2, :], ACT.Copy)
                        for s in range(2):
                            col = bass.ds(f + s * FT, 1)
                            cv = nc.scalar.activation(cb[:, i, s, :], ps[:, bank + s, :], ACT.Identity,
                                                      bias=cbias[:, col], scale=cw[2][:, col])
                        cv.then_inc(S["u_copied"], 1)
                        act.wait_ge(S["conv_done"], at("conv_done", b, f + 1))
                        act.wait_ge(S["halo_kept"], at("halo_kept", b, f + 1))
                        nc.scalar.activation(ub[:, i, 0, 2:2 + T], cb[:, i, 0, :], ACT.Tanh, scale=0.5
                                             ).then_inc(S["tanh_done"], 1)

            def down(b, n, u, g, h, k0, k1):
                for k in range(k1 - k0):
                    split(n, u, k)

            def store(b, n, u):
                for t in range(NT):
                    act.wait_ge(S["y_added"], at("y_added", b, 28 + t + 1))
                    act.dma_start(out_v[:, bass.ds(b * NT + t, 1), :], res[:, t:t + 1, :]
                                  ).then_inc(S["stored"], 16)

            act.sem_inc(S["u_copied"], START["u_copied"])
            for k in range(RING):
                split(0, 0, k - RING)
            act.wait_ge(const_ready, CONST_READY)
            walk(act, stages_of(norm=norm, turn=turn, pool_in=pool_in, q_in=q_in, kv_in=kv_in, q_turn=q_turn, k_turn=k_turn,
                                scores=scores, spread=spread, mix=mix, out=out_proj, up=up, down=down,
                                store=store))
            act.wait_ge(S["stored"], at("stored", NB - 1, 16 * NT))

        @block.vector
        def _(dve):
            v = nc.vector

            def split(n, u, k):
                m, r, s = k + RING, (u + k + RING) % RAW, (u + k + RING) % RING
                if isinstance(n, int) and n + m >= N_ALL:
                    return
                dve.wait_ge(split_hi, n + (m + 1))
                v.tensor_tensor(w_lo[:, s, :], raw[:, r, :], as_f32(w_hi[:, s, :]), ALU.subtract
                                ).then_inc(split_lo, 1)

            def tile_done(name, b, k, n, units, t):
                if t < NT - 1:
                    dve.wait_ge(S[name], at(name, b, k))
                else:
                    dve.wait_ge(unit_used, n + units)

            def turn(a, n, u, i):
                for dt in range(KT):
                    dve.wait_ge(S["hT_hi_done"], at("hT_hi_done", a, 8 * i + dt + 1))
                    v.scalar_tensor_tensor(hT_lo[:, dt, :], ps[:, TURN_BANK[i][dt // 4] + dt % 4, :],
                                           gain[i][:, dt:dt + 1], as_f32(hT_hi[:, dt, :]),
                                           ALU.mult, ALU.subtract).then_inc(S["hT_lo_done"], 1)

            STEP0 = (0, 3, 7, 12)

            def window(a, g):
                dve.wait_ge(S["p_copied"], at("p_copied", a, g + 1))
                step, p_g = STEP0[g], pbuf[:, g, :]
                src, lag = p_g, 1
                for k in range(g + 1):
                    lo = 2 * lag - 1
                    dst = sums[:, k % 2, :]
                    v.tensor_tensor(dst[:, lo:], src[:, lo:], src[:, lo - lag:T + CARRY - lag], ALU.add
                                    ).then_inc(S["win_step"], 1)
                    step += 1
                    dve.wait_ge(S["win_step"], at("win_step", a, step))
                    src, lag = dst, 2 * lag
                if first_block(a):
                    v.tensor_tensor(src[:, CARRY:2 * CARRY], src[:, CARRY:2 * CARRY], ratio[:, g, :], ALU.mult
                                    ).then_inc(const_step, 1)
                    dve.wait_ge(const_step, CONST_STEP + g + 1)
                v.scalar_tensor_tensor(p_g[:, CARRY:], src[:, CARRY:], 1.0 / WINDOWS[g], p_g[:, CARRY:],
                                       ALU.mult, ALU.subtract).then_inc(S["win_step"], 1)
                step += 1
                if g >= MIX:
                    dve.wait_ge(S["pool_done"], at("pool_done", a, g - MIX + 1))
                dve.wait_ge(S["win_step"], at("win_step", a, step))
                v.tensor_copy(mix_hi[:, g % MIX, :], p_g[:, CARRY:]).then_inc(S["win_step"], 1)

            def window_end(a, g):
                dve.wait_ge(S["win_step"], at("win_step", a, STEP0[g] + g + 3))
                v.tensor_tensor(mix_lo[:, g % MIX, :], pbuf[:, g, CARRY:], as_f32(mix_hi[:, g % MIX, :]), ALU.subtract
                                ).then_inc(S["mix_ready"], 1)

            def pool_in(a, n, u):
                for g in range(4):
                    split(n, u, g)
                    if g > 0:
                        window(a, g - 1)
                        window_end(a, g - 1)

            def q_in(a, n, u):
                def summed(t):
                    dve.wait_ge(S["q_squared"], at("q_squared", a, t + 1))
                    v.tensor_reduce(ss_q[:, t, :], xs[:, t, 0:QC].rearrange("p (h d) -> p h d", h=8),
                                    AX.X, ALU.add).then_inc(S["q_summed"], 1)

                def scaled(t):
                    dve.wait_ge(S["q_rstd"], at("q_rstd", a, t + 1))
                    v.tensor_tensor(xs[:, t, 0:QC].rearrange("p (j v d) -> p v j d", v=2, j=4),
                                    ps[:, Q_BANK + t, :].rearrange("p (v j d) -> p v j d", v=2, j=4),
                                    rs_q[:, t, :].rearrange("p (v j) -> p v j", v=2).unsqueeze(3)
                                    .broadcast_to([P, 2, 4, HD]), ALU.mult
                                    ).then_inc(S["q_scaled"], 1)

                window(a, 3)
                window_end(a, 3)
                for k in range(4):
                    split(n, u, k)
                for t in range(NT):
                    summed(t)
                    if t:
                        scaled(t - 1)
                scaled(NT - 1)

            def kv_in(a, n, u):
                split(n, u, 0)
                split(n, u, 1)

                def pair(ap):
                    return ap.rearrange("p t (h d) -> p t h d", h=2)

                def k_of(r):
                    return xs[:, 2 * r:2 * r + 2, QC:QC + KVC]

                for r in range(2):
                    dve.wait_ge(S["k_squared"], at("k_squared", a, r + 1))
                    v.tensor_reduce(ss_k[:, 2 * r:2 * r + 2, :], pair(k_of(r)), AX.X, ALU.add
                                    ).then_inc(S["k_summed"], 1)
                for r in range(2):
                    dve.wait_ge(S["k_rstd"], at("k_rstd", a, r + 1))
                    k_in = ps[:, KV_BANK + r, :].rearrange("p (t s n) -> p t s n", t=2, s=2)[:, :, 0, :]
                    v.tensor_tensor(pair(k_of(r)), pair(k_in),
                                    rs_k[:, 2 * r:2 * r + 2, :].unsqueeze(3).broadcast_to([P, 2, 2, HD]), ALU.mult
                                    ).then_inc(S["k_scaled"], 1)
                dve.wait_ge(S["m_copied"], at("m_copied", a, 4))
                for g in range(4):
                    v.tensor_copy(hT_hi[:, 4 + g, :], mf[:, g, :]).then_inc(S["mT_step"], 1)
                for g in range(4):
                    dve.wait_ge(S["mT_step"], at("mT_step", a, g + 1))
                    v.tensor_tensor(hT_lo[:, 4 + g, :], mf[:, g, :], as_f32(hT_hi[:, 4 + g, :]), ALU.subtract
                                    ).then_inc(S["mT_ready"], 1)

            def inverse(a, t):
                dve.wait_ge(S["exp_done"], at("exp_done", a, t + 1))
                v.tensor_tensor(row_sum[:, t, :], row_sum[:, t, :], sink_exp[:, t, :], ALU.add
                                ).then_inc(S["sm_step"], 1)
                dve.wait_ge(S["sm_step"], at("sm_step", a, SM_INV[t]))
                v.reciprocal(row_sum[:, t, :], row_sum[:, t, :]).then_inc(S["inv_ready"], 1)

            SM_S, SM_INV = (0, 2, 6, 8), (5, 6, 11, 12)

            def scores(a, n, u, t):
                bank = SCORE_BANK[t]
                dve.wait_ge(S["score_done"], at("score_done", a, t + 1))
                if first_block(a) and t == 0:
                    for h in range(2):
                        v.memset(ps[:, bank + h, 0:2 * P].rearrange("p (j c k) -> p j c k", j=2, c=2)[:, :, 1, :],
                                 NEG).then_inc(const_step, 1)
                    dve.wait_ge(const_step, CONST_STEP + 6)
                v.tensor_reduce(mx[:, t, :].rearrange("p (v i) -> p v i", v=2),
                                ps[:, bank:bank + 2, :].rearrange("p v (i k) -> p v i k", i=4),
                                AX.X, ALU.max).then_inc(S["sm_step"], 1)
                dve.wait_ge(S["sm_step"], at("sm_step", a, SM_S[t] + 1))
                v.scalar_tensor_tensor(shift[:, t, :], mx[:, t, :], -1.0, neg_sink[:], ALU.mult, ALU.min
                                       ).then_inc(S["sm_step"], 1)
                dve.wait_ge(S["sm_step"], at("sm_step", a, SM_S[t] + 2))
                v.tensor_tensor(sink_exp[:, t, :], sink[:], shift[:, t, :], ALU.add
                                ).then_inc(S["shift_ready"], 1)
                if t == 1:
                    inverse(a, 0)
                    inverse(a, 1)
                if t == 3:
                    inverse(a, 2)

            def mix(a, n, u, t):
                dve.wait_ge(S["aT_hi_done"], at("aT_hi_done", a, t + 1))
                v.tensor_tensor(hT_lo[:, 0:4, t * P:(t + 1) * P],
                                ps[:, SCORE_BANK[t], :].rearrange("p (j q) -> p j q", j=4),
                                as_f32(hT_hi[:, 0:4, t * P:(t + 1) * P]), ALU.subtract
                                ).then_inc(S["aT_lo_done"], 1)
                if t == 1:
                    inverse(a, 3)

            def out_proj(a, n, u, h, k0, k1):
                for k in range(k1 - k0 - (k1 == 4)):
                    split(n, u, k)
                if k1 < 4:
                    return
                for t in range(NT):
                    tile_done("out_done", a, 3 * h + t + 1, n, k1 - k0, t)
                    c = slice(h * 512, (h + 1) * 512)
                    v.tensor_tensor(x_a[:, t, c], ps[:, OUT_BANK[h] + t, :], x_a[:, t, c], ALU.add
                                    ).then_inc(S["out_added"], 1)
                split(n, u, k1 - k0 - 1)

            def up(b, n, u, f0, count):
                with dve.Fori(0, count // 2) as j:
                    for i in range(2):
                        f = j * 2 + (f0 + i)
                        split(n + j * 4, u, 2 * i)
                        split(n + j * 4, u, 2 * i + 1)
                        dve.wait_ge(S["u_copied"], at("u_copied", b, f + 1))
                        dve.wait_ge(S["halo_in"], at("halo_in", b, f + 1))
                        for tap in (1, 0):
                            for s in range(2):
                                if tap == 0:
                                    dve.wait_ge(S["conv_step"], at("conv_step", b, f * 2 + (s + 1)))
                                st = v.scalar_tensor_tensor(cb[:, i, s, :], ub[:, i, s, tap:tap + T],
                                                            cw[tap][:, bass.ds(f + s * FT, 1)],
                                                            cb[:, i, s, :], ALU.mult, ALU.add)
                                if tap == 1:
                                    st.then_inc(S["conv_step"], 1)
                        st.then_inc(S["conv_done"], 1)
                        gate, value = cb[:, i, 0, :], cb[:, i, 1, :]
                        dve.wait_ge(S["tanh_done"], at("tanh_done", b, f + 1))
                        v.scalar_tensor_tensor(gate, ub[:, i, 0, 2:2 + T], 1.0, gate, ALU.add, ALU.mult
                                               ).then_inc(S["silu_step"], 1)
                        dve.wait_ge(S["silu_step"], at("silu_step", b, f * 3 + 1))
                        v.scalar_tensor_tensor(value, gate, 0.5, value, ALU.mult, ALU.mult
                                               ).then_inc(S["silu_step"], 1)
                        dve.wait_ge(S["silu_step"], at("silu_step", b, f * 3 + 2))
                        g_slot = bass.ds(j * 2 + i, 1)
                        v.tensor_copy(g_hi[:, g_slot, :], value.unsqueeze(1)).then_inc(S["silu_step"], 1)
                        dve.wait_ge(S["silu_step"], at("silu_step", b, f * 3 + 3))
                        v.tensor_tensor(g_lo[:, g_slot, :], value.unsqueeze(1), as_f32(g_hi[:, g_slot, :]),
                                        ALU.subtract).then_inc(S["g_ready"], 1)

            def down(b, n, u, g, h, k0, k1):
                if (g, h) == (0, 0):
                    dve.wait_ge(S["res_copied"], at("res_copied", b, 1))
                last = k1 == GROUPS[g] // 2
                for k in range(k1 - k0 - last):
                    split(n, u, k)
                if not last:
                    return
                for t in range(NT):
                    tile_done("down_done", b, 3 * (2 * g + h) + t + 1, n, k1 - k0, t)
                    c = slice(h * 512, (h + 1) * 512)
                    v.tensor_tensor(res[:, t, c], ps[:, DOWN_BANK[g, h] + t, :], res[:, t, c], ALU.add
                                    ).then_inc(S["y_added"], 1)
                split(n, u, k1 - k0 - 1)

            dve.sem_inc(S["g_ready"], START["g_ready"])
            for k in range(RING):
                split(0, 0, k - RING)
            dve.wait_ge(const_in, CONST_IN)
            sink_of = sink_row[:].rearrange("p (v j i) -> p i v j", v=2, j=2)
            for i in range(2):
                half = slice(i * HD, (i + 1) * HD)
                for c in range(2):
                    v.tensor_copy(sink[half, :].rearrange("p (v c j) -> p c v j", v=2, c=2)[:, c],
                                  sink_of[half, i]).then_inc(const_step, 1)
            v.tensor_copy(pw_hi[:], pw_in).then_inc(const_step, 1)
            v.tensor_scalar(gk[:], gk_in[:], HD ** -0.5, None, ALU.mult).then_inc(const_ready, 1)
            dve.wait_ge(const_turned, 1)
            v.tensor_copy(cst[:], ps[:, 0, 0:200]).then_inc(const_step, 1)
            dve.wait_ge(const_step, 6)
            v.tensor_scalar(neg_sink[:], sink[:], -1.0, None, ALU.mult).then_inc(const_ready, 1)
            v.tensor_tensor(pw_lo[:], pw_in, as_f32(pw_hi[:]), ALU.subtract).then_inc(const_ready, 1)
            v.tensor_tensor(pbias[:], pbias_in, pscale, ALU.mult).then_inc(const_ready, 1)
            dve.wait_ge(const_pool, CONST_POOL)
            walk(dve, stages_of(turn=turn, pool_in=pool_in, q_in=q_in, kv_in=kv_in,
                                scores=scores, mix=mix, out=out_proj, up=up, down=down))

        @block.gpsimd
        def _(pool):
            g = nc.gpsimd

            def wait(semaphore, value):
                pool.wait_ge(semaphore, value)
                if not isinstance(value, int):
                    pool.sem_inc(pool_waited, 1)

            def inverse_root(dst, src, count, width, step, k_step, done):
                g.tensor_scalar(dst, src, 1.0 / width, EPS, ALU.mult, ALU.add).then_inc(S[step], 1)
                wait(S[step], k_step)
                g.tensor_tensor(dst, dst, half_neg[:, 0:count], ALU.pow).then_inc(S[done], 1)

            def norm(a, n, u, i, only=None):
                for t in range(NT) if only is None else (only,):
                    wait(S["sq_done"], at("sq_done", a, 4 * i + t + 1))
                    inverse_root(rstd[:, t:t + 1], ss[:, t:t + 1], 1, D, "rstd_step",
                                 at("rstd_step", a, 4 * i + t + 1), "rstd_done")
                if i == 0 and only == 0:
                    if not first_block(a):
                        wait(S["mix_done"], at("mix_done", a - 1, 4))
                    g.tensor_copy(v_even[:, 0, :], v_even[:, NT, :]).then_inc(S["v_kept"], 1)

            def q_in(a, n, u):
                for t in range(NT):
                    wait(S["q_summed"], at("q_summed", a, t + 1))
                    inverse_root(rs_q[:, t, :], ss_q[:, t, :], 8, HD, "q_step", at("q_step", a, t + 1), "q_rstd")

            def kv_in(a, n, u):
                for r in range(2):
                    wait(S["k_summed"], at("k_summed", a, r + 1))
                    inverse_root(rs_k[:, 2 * r:2 * r + 2, :].rearrange("p t h -> p (t h)"),
                                 ss_k[:, 2 * r:2 * r + 2, :].rearrange("p t h -> p (t h)"),
                                 4, HD, "k_step", at("k_step", a, r + 1), "k_rstd")

            def scale_probs(a, t):
                wait(S["inv_ready"], at("inv_ready", a, t + 1))
                pr = xs[:, t, :].rearrange("p (i k) -> p i k", i=8)
                g.tensor_tensor(pr, pr, row_sum[:, t, :].unsqueeze(2).broadcast_to([P, 8, P]), ALU.mult
                                ).then_inc(S["p_scaled"], 1)

            def scores(a, n, u, t):
                if t == 1:
                    scale_probs(a, 0)
                    scale_probs(a, 1)
                if t == 3:
                    scale_probs(a, 2)

            def mix(a, n, u, t):
                if t == 1:
                    scale_probs(a, 3)

            def up(b, n, u, f0, count):
                with pool.Fori(0, count // 2) as j:
                    for i in range(2):
                        f = j * 2 + (f0 + i)
                        wait(S["g_ready"], at("g_ready", b, f - 1))
                        g.tensor_copy(ub[:, i, :, 0:2], halo[:, bass.ds(f, 1), :, :].squeeze(1)
                                      ).then_inc(S["halo_in"], 1)
                        wait(S["u_copied"], at("u_copied", b, f + 1))
                        wait(S["halo_in"], at("halo_in", b, f + 1))
                        g.tensor_copy(halo[:, bass.ds(f, 1), :, :].squeeze(1), ub[:, i, :, T:T + 2]
                                      ).then_inc(S["halo_kept"], 1)

            def keep(a, n, u):
                if not first_block(a):
                    wait(S["stored"], at("stored", a - 1, 16 * NT))
                wait(S["out_added"], at("out_added", a, 8))
                g.tensor_copy(res[:], x_a[:]).then_inc(S["res_copied"], 1)

            g.memset(ident[:], 0.0).then_inc(const_cleared, 1)
            g.memset(ratio[:], 1.0).then_inc(const_cleared, 1)
            wait(const_cleared, 2)
            g.affine_select(out=ident[:], in_=ident[:], compare_op=ALU.not_equal, fill=1.0, base=0,
                            pattern=[[-1, P]], channel_multiplier=1).then_inc(const_pool, 1)
            for i, w in enumerate(WINDOWS):
                for pos in range(w - 1):
                    ms = g.memset(ratio[:, i, pos:pos + 1], float(w) / (pos + 1))
            ms.then_inc(const_pool, 1)
            g.memset(half_neg[:], -0.5).then_inc(const_pool, 1)
            for ap in (k_keep[:], v_even[:], p_keep[:], halo[:]):
                g.memset(ap, 0.0).then_inc(const_pool, 1)
            wait(const_pool, CONST_POOL)
            walk(pool, stages_of(norm=norm, q_in=q_in, kv_in=kv_in, scores=scores, mix=mix, up=up, keep=keep))


_INS = ["x", "norm1_g", "w_in", "q_norm_g", "k_norm_g", "attn_sinks", "pool_w", "pool_b", "pool_scale",
        "w_out", "norm2_g", "w_up", "conv_w", "conv_b", "w_down"]
_OUTS = [((1, SEQ, D), "float32")]


def kernel(**inputs):
    import numpy as _np
    import concourse.bacc as _bacc
    from concourse import mybir as _mybir
    from concourse.bass_utils import run_bass_kernel_spmd as _run

    nc = _bacc.Bacc("TRN2", target_bir_lowering=False, num_devices=1)
    arrays, args = {}, []
    for name in _INS:
        a = _np.ascontiguousarray(inputs[name])
        arrays[f"in_{name}_dram"] = a
        args.append(nc.dram_tensor(f"in_{name}_dram", a.shape, _mybir.dt.from_np(a.dtype), kind="ExternalInput").ap())
    for i, (shape, dtype) in enumerate(_OUTS):
        dt = _mybir.dt.from_np(_np.dtype(dtype))
        args.append(nc.dram_tensor(f"out_{i}_dram", shape, dt, kind="ExternalOutput").ap())
    bass_hybrid_block(nc, *args)
    r = _run(nc, [arrays], core_ids=[0])
    got = tuple(r.results[0][f"out_{i}_dram"] for i in range(len(_OUTS)))
    return got[0]
```

```python
from contextlib import ExitStack

import concourse.bass as bass
from concourse import mybir

ALU = mybir.AluOpType
ACT = mybir.ActivationFunctionType
AX = mybir.AxisListType
F32 = mybir.dt.float32
F32R = mybir.dt.float32r

P = 128
T = 512
NT = T // P
D = 1024
KT = D // P
SEQ = 2048
NB = SEQ // T
HD = 64
QC = 512
KVC = 128
FF = 2816
FT = FF // P
WINDOWS = (2, 4, 8, 16)
CARRY = 16
EPS = 1e-6
NEG = -1e30

UNIT = 1024
RAW = 2
MIX = 2
RING = 4
GROUPS = (8, 6, 4, 4)
BASE = (0, 8, 14, 18)

ITERATION = [
    ("F", "up", (0, 8), 16), ("F", "down", (0, 0, 0, 4), 4), ("F", "down", (0, 1, 0, 4), 4),
    ("F", "up", (8, 6), 12), ("F", "down", (1, 0, 0, 1), 1), ("A", "norm", (0, 0), 0),
    ("F", "down", (1, 0, 1, 2), 1), ("A", "norm", (0, 1), 0),
    ("F", "down", (1, 0, 2, 3), 1), ("A", "norm", (0, 2), 0),
    ("F", "down", (1, 1, 0, 1), 1), ("A", "norm", (0, 3), 0), ("F", "down", (1, 1, 1, 3), 2),
    ("F", "up", (14, 8), 16), ("F", "down", (2, 0, 0, 2), 2),
    ("A", "turn", (0,), 0), ("A", "pool_in", (), 4), ("A", "pool_map", (0,), 0), ("A", "q_in", (0, 1), 1),
    ("A", "pool_map", (1,), 0), ("A", "q_in", (1, 2), 1), ("A", "pool_map", (2,), 0), ("A", "q_in", (2, 3), 1),
    ("A", "pool_map", (3,), 0), ("A", "q_in", (3, 4), 1), ("A", "kv_in", (0, 1), 1),
    ("A", "q_turn", (), 0), ("A", "kv_in", (1, 2), 1), ("A", "join", (), 0),
    ("F", "down", (2, 1, 0, 1), 1), ("A", "k_turn", (), 0), ("F", "down", (2, 1, 1, 2), 1),
    ("A", "scores", (0,), 0), ("A", "scores", (1,), 0), ("F", "down", (3, 0, 0, 2), 2),
    ("A", "spread", (0,), 0), ("A", "spread", (1,), 0), ("A", "scores", (2,), 0), ("A", "scores", (3,), 0),
    ("A", "mix", (0,), 0), ("A", "mix", (1,), 0), ("A", "out", (0, 0, 1), 1),
    ("A", "spread", (2,), 0), ("A", "out", (0, 1, 2), 1), ("A", "spread", (3,), 0),
    ("A", "mix", (2,), 0), ("A", "mix", (3,), 0), ("A", "out", (0, 2, 4), 2), ("A", "out", (1, 0, 4), 4),
    ("A", "norm", (1,), 0), ("F", "down", (3, 1, 0, 2), 2), ("A", "turn", (1,), 0),
    ("F", "store", (), 0),
]
PROLOGUE = [("A", name, args, units) for name, args, units in [
    ("norm", (0,), 0), ("turn", (0,), 0), ("pool_in", (), 4), ("pool_map", (0,), 0), ("pool_map", (1,), 0),
    ("kv_in", (0, 1), 1), ("pool_map", (2,), 0), ("kv_in", (1, 2), 1), ("pool_map", (3,), 0),
    ("q_in", (0, 1), 1), ("k_turn", (), 0), ("q_in", (1, 4), 3), ("q_turn", (), 0), ("join", (), 0),
    ("scores", (0,), 0), ("scores", (1,), 0), ("scores", (2,), 0), ("scores", (3,), 0),
    ("spread", (0,), 0), ("spread", (1,), 0), ("mix", (0,), 0), ("mix", (1,), 0), ("out", (0, 0, 1), 1),
    ("spread", (2,), 0), ("out", (0, 1, 2), 1), ("spread", (3,), 0),
    ("mix", (2,), 0), ("mix", (3,), 0), ("out", (0, 2, 4), 2), ("out", (1, 0, 4), 4),
    ("norm", (1,), 0), ("turn", (1,), 0)]]
EPILOGUE = [s for s in ITERATION if s[0] == "F"]
N_PRO = sum(s[3] for s in PROLOGUE)
N_ITER = sum(s[3] for s in ITERATION)
N_ALL = N_PRO + (NB - 1) * N_ITER + sum(s[3] for s in EPILOGUE)
assert N_ITER % RING == 0 and N_ITER % RAW == 0

UP_BANK = {0: 0, 8: 4, 14: 4}
DOWN_BANK = {(0, 0): 4, (0, 1): 0, (1, 0): 0, (1, 1): 0, (2, 0): 0, (2, 1): 0, (3, 0): 0, (3, 1): 4}
TURN_BANK = ((4, 0), (0, 4))
POOL_BANK, Q_TURN_BANK = 4, 0
SCORE_BANK = (4, 6, 0, 2)
OUT_BANK = (4, 0)

PER = dict(
    sq_done=8, rstd_step=8, rstd_done=8, xs_ready=8, turned=16, hT_hi_done=16, hT_lo_done=16,
    p_carried=4, p_copied=4, win_step=18, mix_ready=4, pool_done=4, m_copied=4, mT_step=4, mT_ready=4,
    q_done=3, q_squared=4, q_summed=4, q_step=4, q_rstd=4, q_scaled=4,
    kv_done=1, k_squared=2, k_summed=2, k_step=2, k_rstd=2, k_scaled=2, v_kept=1,
    kT_done=1, k_placed=1, kT_ready=1, qT_done=4, qT_ready=4,
    score_done=4, sm_step=12, shift_ready=4, exp_done=4, inv_ready=4, p_scaled=4,
    spread_done=4, PT_ready=4, mix_done=4, aT_hi_done=4, aT_lo_done=4,
    out_done=6, out_added=8, res_copied=1,
    u_copied=FT, halo_in=FT, halo_kept=FT, conv_step=2 * FT, conv_done=FT, tanh_done=FT, silu_step=3 * FT,
    g_ready=FT, down_done=24, y_added=32, stored=16 * NT,
)
START = dict(u_copied=2, g_ready=2, stored=1)


def banks(first):
    return (4, 0, 2) if first else (0, 4, 6)


def at(name, block, k):
    return block * PER[name] + (k + START.get(name, 0))


def bass_hybrid_block(nc, x, norm1_g, w_in, q_norm_g, k_norm_g, attn_sinks, pool_w, pool_b, pool_scale,
                      w_out, norm2_g, w_up, conv_w, conv_b, w_down, out):
    x_v = x[0].rearrange("(t p) d -> p t d", p=P)
    out_v = out[0].rearrange("(t p) d -> p t d", p=P)
    w_in_v = w_in[0].rearrange("(k p) n -> p k n", p=P)
    w_out_v = w_out[0].rearrange("(k p) n -> p k n", p=P)
    w_up_v = w_up[0].rearrange("(k p) n -> p k n", p=P)
    w_down_v = w_down[0].rearrange("(k p) n -> p k n", p=P)

    with ExitStack() as ctx:
        def sb(name, shape, dt=F32):
            return ctx.enter_context(nc.sbuf_tensor(name, shape, dt))

        def sem(name):
            return ctx.enter_context(nc.semaphore(name))

        raw = sb("raw", [P, RAW, UNIT])
        w_hi = sb("w_hi", [P, RING, UNIT], F32R)
        w_lo = sb("w_lo", [P, RING, UNIT], F32R)
        x_a = sb("x_a", [P, NT, D])
        res = sb("res", [P, NT, D])
        xs = sb("xs", [P, NT, D])
        hT_hi = sb("hT_hi", [P, KT, T], F32R)
        hT_lo = sb("hT_lo", [P, KT, T], F32R)
        g_hi = sb("g_hi", [P, 8, T], F32R)
        g_lo = sb("g_lo", [P, 8, T], F32R)
        qT = sb("qT", [P, NT, T])
        PT = sb("PT", [P, 2, 2, 4, P])
        kT = sb("kT", [P, NT, 2, 2, HD])
        k_keep = sb("k_keep", [P, HD])
        v_odd = sb("v_odd", [P, NT, KVC])
        v_even = sb("v_even", [P, NT + 1, KVC])
        mix_hi = sb("mix_hi", [P, MIX, T], F32R)
        mix_lo = sb("mix_lo", [P, MIX, T], F32R)
        pw_hi = sb("pw_hi", [P, 4, P], F32R)
        pw_lo = sb("pw_lo", [P, 4, P], F32R)
        work = sb("work", [P, 2 * 2 * (T + 2) + 2 * 2 * T])
        ub = work[:, 0:2056].rearrange("p (r s t) -> p r s t", r=2, s=2)
        cb = work[:, 2056:4104].rearrange("p (r s t) -> p r s t", r=2, s=2)
        pbuf = work[:, 0:4 * (T + CARRY)].rearrange("p (g t) -> p g t", g=4)
        mf = pbuf[:, :, CARRY:]
        sums = work[:, 4 * (T + CARRY):6 * (T + CARRY)].rearrange("p (r t) -> p r t", r=2)
        p_keep = sb("p_keep", [P, 4, CARRY])
        halo = sb("halo", [P, FT, 2, 2])
        cst = sb("cst", [P, 200])
        cw = [cst[:, 0:44], cst[:, 44:88], cst[:, 112:156]]
        cbias = cst[:, 156:200]
        gain = [cst[:, 88:96], cst[:, 96:104]]
        pbias_in, pscale = cst[:, 104:108], cst[:, 108:112]
        pbias = sb("pbias", [P, 4])
        gq = sb("gq", [P, 1])
        gk_in = sb("gk_in", [P, 1])
        gk = sb("gk", [P, 1])
        sink_row = sb("sink_row", [P, 8])
        sink = sb("sink", [P, 8])
        neg_sink = sb("neg_sink", [P, 8])
        half_neg = sb("half_neg", [P, 8])
        ident = sb("ident", [P, P])
        ss = sb("ss", [P, NT])
        rstd = sb("rstd", [P, NT])
        ss_q = sb("ss_q", [P, NT, 8])
        rs_q = ss_q
        ss_k = sb("ss_k", [P, NT, 2])
        rs_k = sb("rs_k", [P, NT, 2])
        mx = sb("mx", [P, NT, 8])
        shift = sb("shift", [P, NT, 8])
        sink_exp = sb("sink_exp", [P, NT, 8])
        row_sum = sb("row_sum", [P, NT, 8])
        ps = ctx.enter_context(nc.psum_tensor("ps", [P, 8, 512], F32))

        S = {name: sem(name) for name in PER}
        x_loaded = [sem(f"x_loaded{t}") for t in range(NT)]
        raw_in = [sem(f"raw_in{i}") for i in range(RAW)]
        split_hi, split_lo, unit_used = sem("split_hi"), sem("split_lo"), sem("unit_used")
        vectors_in, vectors_read = sem("vectors_in"), sem("vectors_read")
        const_in, const_pool, const_cleared = sem("const_in"), sem("const_pool"), sem("const_cleared")
        sp_waited, pe_waited, pool_waited = sem("sp_waited"), sem("pe_waited"), sem("pool_waited")
        const_turned, const_step, const_ready = sem("const_turned"), sem("const_step"), sem("const_ready")

        ratio = res[:, 2, 0:4 * CARRY].rearrange("p (g t) -> p g t", g=4)
        vec_rows = res[:, 0, 0:256].rearrange("p (a n) -> p a n", a=2)
        pw_in = res[:, 1, 0:512].rearrange("p (g n) -> p g n", g=4)

        def as_f32(ap):
            return ap.bitcast(F32)

        def walk(engine, stages):
            def run(order, block_f, block_a, n, u):
                for side, name, args, units in order:
                    stages[name](block_a if side == "A" else block_f, n, u, *args)
                    n, u = n + units, u + units
            run(PROLOGUE, None, 0, 0, 0)
            with engine.Fori(0, NB - 1) as it:
                run(ITERATION, it, it + 1, it * N_ITER + N_PRO, N_PRO)
            run(EPILOGUE, NB - 1, None, N_PRO + (NB - 1) * N_ITER, N_PRO)

        def last_block(b):
            return isinstance(b, int) and b == NB - 1

        def first_block(a):
            return isinstance(a, int) and a == 0

        def stages_of(**have):
            names = {s[1] for s in ITERATION}
            return {name: have.get(name, lambda *_: None) for name in names}

        def deferred(b, g, h):
            return 0 if last_block(b) else {(2, 0): 1, (3, 1): 2}.get((g, h), 0)

        VECTORS_IN, CONST_IN = 7 * 16, 6 * 16
        CONST_POOL = 7
        CONST_STEP, CONST_READY = 5, 4

        block = ctx.enter_context(nc.Block())

        @block.sync
        def _(sp):
            def load(n, u, k, src):
                r = (u + k) % RAW
                if not isinstance(n, int) or n + k >= RAW:
                    sp.wait_ge(split_lo, n + (k - RAW + 1))
                    if not isinstance(n, int):
                        sp.sem_inc(sp_waited, 1)
                sp.dma_start(raw[:, r, :].rearrange("p (k n) -> p k n", k=src.shape[1]), src).then_inc(raw_in[r], 16)

            def load_x(a):
                if not first_block(a):
                    sp.wait_ge(S["xs_ready"], at("xs_ready", a - 1, 8))
                    sp.sem_inc(sp_waited, 1)
                    sp.wait_ge(S["res_copied"], at("res_copied", a - 1, 1))
                    sp.sem_inc(sp_waited, 1)
                for t in range(NT):
                    tile = slice(a * NT + t, a * NT + t + 1) if isinstance(a, int) else bass.ds(a * NT + t, 1)
                    sp.dma_start(x_a[:, t:t + 1, :], x_v[:, tile, :]).then_inc(x_loaded[t], 16)

            def up(b, n, u, f0, count):
                with sp.Fori(0, count // 2) as j:
                    for i in range(4):
                        col = j * (2 * P) + ((f0 + i // 2) * P + (i % 2) * FF)
                        load(j * 4 + n, u, i, w_up_v[:, :, bass.ds(col, P)])

            def down(b, n, u, g, h, k0, k1):
                for k in range(k0, k1):
                    kt = BASE[g] + 2 * k
                    load(n, u, k - k0, w_down_v[:, kt:kt + 2, h * 512:(h + 1) * 512])
                if (g, h) == (0, 1) and not last_block(b):
                    load_x(b + 1)

            def pool_in(a, n, u):
                for g in range(4):
                    c = QC + 2 * KVC + g * P
                    load(n, u, g, w_in_v[:, :, c:c + P])
                    if first_block(a) and g == RAW - 1:
                        load_constants()

            def q_in(a, n, u, k0, k1):
                for k in range(k0, k1):
                    load(n, u, k - k0, w_in_v[:, 2 * k:2 * k + 2, 0:QC])

            def kv_in(a, n, u, k0, k1):
                for k in range(k0, k1):
                    load(n, u, k - k0, w_in_v[:, 4 * k:4 * k + 4, QC:QC + 2 * KVC])

            def out_proj(a, n, u, h, k0, k1):
                for k in range(k0, k1):
                    kt = (4 + 2 * k) % KT
                    load(n, u, k - k0, w_out_v[:, kt:kt + 2, h * 512:(h + 1) * 512])

            def load_constants():
                for i in range(2):
                    half = slice(i * HD, (i + 1) * HD)
                    sp.dma_start(gq[half, :], q_norm_g.rearrange("o d -> d o")).then_inc(const_in, 16)
                    sp.dma_start(gk_in[half, :], k_norm_g.rearrange("o d -> d o")).then_inc(const_in, 16)
                sp.dma_start(sink_row[:], attn_sinks[0:1, :].broadcast_to([P, 8])).then_inc(const_in, 16)
                sp.dma_start(pw_in, pool_w[0].rearrange("g c d -> c g d")).then_inc(const_in, 16)

            load_x(0)
            for row, a, src in [(0, 0, conv_w[0, 0:2].rearrange("c (f p) -> (c f) p", p=P)),
                                (88, 0, norm1_g[0].rearrange("(f p) -> f p", p=P)),
                                (96, 0, norm2_g[0].rearrange("(f p) -> f p", p=P)),
                                (104, 0, pool_b[0]), (108, 0, pool_scale[0].rearrange("(f p) -> f p", p=P)),
                                (0, 1, conv_w[0, 2].rearrange("(f p) -> f p", p=P)),
                                (44, 1, conv_b[0].rearrange("(f p) -> f p", p=P))]:
                sp.dma_start(vec_rows[row:row + src.shape[0], a, :], src).then_inc(vectors_in, 16)
            walk(sp, stages_of(up=up, down=down, pool_in=pool_in, q_in=q_in, kv_in=kv_in, out=out_proj))

        @block.tensor
        def _(pe):
            def passes(out_ap, l_hi, l_lo, r_hi, r_lo, first, last):
                pe.matmul(out_ap, l_hi, r_hi, start=first, stop=False)
                pe.matmul(out_ap, l_hi, r_lo, start=False, stop=False)
                return pe.matmul(out_ap, l_lo, r_hi, start=False, stop=last)

            def by_token(n, u, k0, k1, units, per_unit, place, left, signal, tile_wait, unit_wait=None,
                         tiles_of_bank=1):
                for k in range(k0, k1):
                    if unit_wait:
                        unit_wait(k)
                    pe.wait_ge(split_lo, n + (k - k0 + 1))
                    s = (u + k - k0) % RING
                    hi = w_hi[:, s, :].rearrange("p (k n) -> p k n", k=per_unit)
                    lo = w_lo[:, s, :].rearrange("p (k n) -> p k n", k=per_unit)
                    done = k == units - 1
                    steps = [(kk, t) for kk in range(per_unit) for t in range(NT)]
                    if done or k == 2:
                        steps = [(kk, t) for t in range(NT) for kk in range(per_unit)]
                    for kk, t in steps:
                        i = k * per_unit + kk
                        if kk == 0:
                            tile_wait(k, t)
                        l_hi, l_lo = left(i, t)
                        mm = passes(place(t), l_hi, l_lo, hi[:, kk, :], lo[:, kk, :],
                                    i == 0 and t % tiles_of_bank == 0,
                                    i == per_unit * units - 1 and (t + 1) % tiles_of_bank == 0)
                        if done and kk == per_unit - 1 and t < NT - 1 and (t + 1) % tiles_of_bank == 0:
                            mm.then_inc(S[signal], 1)
                    mm.then_inc(unit_used, 1)

            def tokens(t):
                return slice(t * P, (t + 1) * P)

            def up(b, n, u, f0, count):
                if f0 == 8:
                    pe.wait_ge(S["y_added"], at("y_added", b, 4))
                    if not isinstance(b, int):
                        pe.sem_inc(pe_waited, 1)
                with pe.Fori(0, count // 2) as j:
                    for i in range(2):
                        bank = UP_BANK[f0] + 2 * i
                        pe.wait_ge(S["u_copied"], at("u_copied", b, j * 2 + (f0 + i - 1)))
                        for s in range(2):
                            pe.wait_ge(split_lo, n + (j * 4 + (2 * i + s + 1)))
                            w = (u + 2 * i + s) % RING
                            for k in range(KT):
                                if f0 == 0 and i == 0 and s == 0:
                                    pe.wait_ge(S["hT_lo_done"], at("hT_lo_done", b, 8 + k + 1))
                                c = slice(k * P, (k + 1) * P)
                                mm = passes(ps[:, bank + s, :], w_hi[:, w, c], w_lo[:, w, c],
                                            hT_hi[:, k, :], hT_lo[:, k, :], k == 0, k == KT - 1)
                            mm.then_inc(unit_used, 1)

            def down(b, n, u, g, h, k0, k1):
                def added(g, h, t):
                    return S["y_added"], at("y_added", b, 4 * (2 * g + h) + t + 1)

                def tile_wait(k, t):
                    if k > 0:
                        return
                    if (g, h) == (0, 1):
                        pe.wait_ge(S["u_copied"], at("u_copied", b, 8))
                    elif (g, h) in ((1, 0), (1, 1), (2, 0)):
                        pe.wait_ge(*added(*{(1, 0): (0, 1), (1, 1): (1, 0), (2, 0): (1, 1)}[g, h], t))
                    elif (g, h) == (2, 1) and not last_block(b):
                        pe.wait_ge(S["qT_ready"], at("qT_ready", b + 1, t + 1))
                    elif (g, h) == (2, 1):
                        pe.wait_ge(*added(2, 0, t))
                    elif (g, h) == (3, 0):
                        pe.wait_ge(*added(2, 1, t))
                    elif (g, h) == (3, 1) and not last_block(b):
                        pe.wait_ge(S["out_added"], at("out_added", b + 1, t + 1))
                    elif (g, h) == (3, 1):
                        pe.wait_ge(S["u_copied"], at("u_copied", b, FT))

                slot0 = {0: 0, 1: 0, 2: 0, 3: 4}[g]
                by_token(n, u, k0, k1, GROUPS[g] // 2, 2, lambda t: ps[:, DOWN_BANK[g, h] + t, :],
                         lambda i, t: (g_hi[:, slot0 + i, tokens(t)], g_lo[:, slot0 + i, tokens(t)]),
                         "down_done", tile_wait,
                         lambda k: pe.wait_ge(S["g_ready"], at("g_ready", b, BASE[g] + 2 * k + 2)))

            def turn_by_tile(a, i):
                if i == 0:
                    pe.wait_ge(vectors_read, 1)
                else:
                    pe.wait_ge(S["out_added"], at("out_added", a, 8))
                for t in range(NT):
                    pe.wait_ge(S["xs_ready"], at("xs_ready", a, 4 * i + t + 1))
                    for dt in range(KT):
                        bank = TURN_BANK[i][dt // 4] + dt % 4
                        mm = pe.transpose(ps[:, bank, tokens(t)], xs[:, t, dt * P:(dt + 1) * P], ident[:])
                        if t == NT - 1:
                            mm.then_inc(S["turned"], 1)

            def turn(a, n, u, i):
                if first_block(a):
                    return turn_by_tile(a, i)
                for dt in range(KT):
                    bank = TURN_BANK[i][dt // 4] + dt % 4
                    if i == 0 and dt < 4:
                        pe.wait_ge(S["u_copied"], at("u_copied", a - 1, FT))
                    elif i == 0:
                        pe.wait_ge(S["y_added"], at("y_added", a - 1, 16 + dt - 3))
                    elif dt < 4:
                        pe.wait_ge(S["out_added"], at("out_added", a, 4 + dt + 1))
                    else:
                        pe.wait_ge(S["y_added"], at("y_added", a - 1, 28 + dt - 3))
                    if dt == 0:
                        pe.wait_ge(S["xs_ready"], at("xs_ready", a, 4 * i + 4))
                    for t in range(NT):
                        mm = pe.transpose(ps[:, bank, tokens(t)], xs[:, t, dt * P:(dt + 1) * P], ident[:])
                    mm.then_inc(S["turned"], 1)

            def pool_in(a, n, u):
                for g in range(4):
                    pe.wait_ge(split_lo, n + (g + 1))
                    w = (u + g) % RING
                    for k in range(KT):
                        if g == 0:
                            pe.wait_ge(S["hT_lo_done"], at("hT_lo_done", a, k + 1))
                        c = slice(k * P, (k + 1) * P)
                        mm = passes(ps[:, POOL_BANK + g, :], w_hi[:, w, c], w_lo[:, w, c],
                                    hT_hi[:, k, :], hT_lo[:, k, :], k == 0, k == KT - 1)
                    mm.then_inc(unit_used, 1)

            def h_left(i, t):
                return hT_hi[:, i, tokens(t)], hT_lo[:, i, tokens(t)]

            def pool_map(a, n, u, g):
                if first_block(a) and g == 0:
                    pe.wait_ge(const_ready, CONST_READY)
                pe.wait_ge(S["mix_ready"], at("mix_ready", a, g + 1))
                pe.wait_ge(S["p_copied"], at("p_copied", a, g + 1))
                passes(ps[:, POOL_BANK + g, :], pw_hi[:, g, :], pw_lo[:, g, :],
                       mix_hi[:, g % MIX, :], mix_lo[:, g % MIX, :], True, True).then_inc(S["pool_done"], 1)

            def q_in(a, n, u, k0, k1):
                def tile_wait(k, t):
                    if k == 0 and first_block(a):
                        pe.wait_ge(S["m_copied"], at("m_copied", a, t + 1))
                by_token(n, u, k0, k1, 4, 2, lambda t: ps[:, banks(first_block(a))[0] + t, :], h_left, "q_done",
                         tile_wait)

            def kv_in(a, n, u, k0, k1):
                bank = banks(first_block(a))[1]

                def tile_wait(k, t):
                    if k == 0 and t % 2 == 0 and not first_block(a):
                        pe.wait_ge(S["m_copied"], at("m_copied", a, t // 2 + 1))
                by_token(n, u, k0, k1, 2, 4,
                         lambda t: ps[:, bank + t // 2, (t % 2) * 2 * KVC:(t % 2 + 1) * 2 * KVC],
                         h_left, "kv_done", tile_wait, tiles_of_bank=2)

            def q_turn(a, n, u):
                for t in range(NT):
                    if first_block(a) and t == 2:
                        pe.wait_ge(S["kT_ready"], at("kT_ready", a, 1))
                    pe.wait_ge(S["q_scaled"], at("q_scaled", a, t + 1))
                    for j in range(4):
                        q_t = ps[:, Q_TURN_BANK + t, :].rearrange("p (c j q) -> p j c q", c=2, j=4)[:, j]
                        mm = pe.transpose(q_t, xs[:, t, j * P:(j + 1) * P], ident[:])
                    mm.then_inc(S["qT_done"], 1)

            def k_turn(a, n, u):
                if not first_block(a):
                    pe.wait_ge(S["m_copied"], at("m_copied", a, 3))
                pe.wait_ge(S["k_scaled"], at("k_scaled", a, 2))
                for t in range(NT):
                    mm = pe.transpose(ps[:, banks(first_block(a))[2], tokens(t)], xs[:, t, QC:QC + KVC], ident[:])
                mm.then_inc(S["kT_done"], 1)

            def scores(a, n, u, t):
                if t == 0:
                    pe.wait_ge(S["qT_ready"], at("qT_ready", a, 4))
                    pe.wait_ge(S["kT_ready"], at("kT_ready", a, 1))
                if t >= 2 and not first_block(a):
                    pe.wait_ge(S["y_added"], at("y_added", a - 1, 24 + 2 * (t - 1)))
                for c in range(2):
                    for j in range(2):
                        q = slice((2 * c + j) * P, (2 * c + j + 1) * P)
                        for v in range(2):
                            rows = slice(v * HD, (v + 1) * HD)
                            mm = pe.matmul(ps[:, SCORE_BANK[t] + v, q], qT[rows, t, q],
                                           kT[rows, t, c].rearrange("p a d -> p (a d)"), start=True, stop=True)
                mm.then_inc(S["score_done"], 1)

            def spread(a, n, u, t):
                pe.wait_ge(S["p_scaled"], at("p_scaled", a, t + 1))
                for i in range(8):
                    mm = pe.transpose(ps[:, SCORE_BANK[t] + i // 4, (i % 4) * P:(i % 4 + 1) * P],
                                      xs[:, t, i * P:(i + 1) * P], ident[:])
                mm.then_inc(S["spread_done"], 1)

            def mix(a, n, u, t):
                pe.wait_ge(S["PT_ready"], at("PT_ready", a, t + 1))
                for v in range(2):
                    d = slice(v * HD, (v + 1) * HD)
                    for c, window in enumerate((v_even, v_odd)):
                        for i in range(2):
                            q = slice(i * HD, (i + 1) * HD)
                            o = ps[q, SCORE_BANK[t], v * 256:(v + 1) * 256] \
                                .rearrange("p (j c q) -> p c j q", j=2, c=2)[:, c]
                            mm = pe.matmul(o, window[:, t, d], PT[:, t % 2, v, 2 * c:2 * c + 2, q],
                                           start=True, stop=True)
                mm.then_inc(S["mix_done"], 1)

            def out_proj(a, n, u, h, k0, k1):
                def left(i, t):
                    return h_left((4 + i) % KT, t)

                def tile_wait(k, t):
                    if h == 0 and k == 0 and t % 2 == 0:
                        pe.wait_ge(S["aT_lo_done"], at("aT_lo_done", a, 1 + t // 2))
                    if h == 0 and k == 2:
                        pe.wait_ge(S["aT_lo_done"], at("aT_lo_done", a, t + 1))

                def unit_wait(k):
                    if h == 0 and k < 2:
                        pe.wait_ge(S["mT_ready"], at("mT_ready", a, 2 * k + 2))
                by_token(n, u, k0, k1, 4, 2, lambda t: ps[:, OUT_BANK[h] + t, :], left, "out_done",
                         tile_wait, unit_wait)

            pe.wait_ge(const_pool, CONST_POOL)
            pe.wait_ge(vectors_in, VECTORS_IN)
            pe.transpose(ps[:, 0, 0:112], vec_rows[0:112, 0, :], ident[0:112, 0:112])
            pe.transpose(ps[:, 0, 112:200], vec_rows[0:88, 1, :], ident[0:88, 0:88]).then_inc(const_turned, 1)
            walk(pe, stages_of(up=up, down=down, turn=turn, pool_in=pool_in, pool_map=pool_map, q_in=q_in,
                               kv_in=kv_in, q_turn=q_turn, k_turn=k_turn, scores=scores, spread=spread, mix=mix, out=out_proj))

        @block.scalar
        def _(act):
            def split(n, u, k):
                m, r, s = k + RING, (u + k + RING) % RAW, (u + k + RING) % RING
                if isinstance(n, int) and n + m >= N_ALL:
                    return
                if not isinstance(n, int) or n + k >= 0:
                    act.wait_ge(unit_used, n + (k + 1))
                act.wait_ge(raw_in[r], (n + m) * (16 // RAW) + (16 - r * (16 // RAW)))
                nc.scalar.activation(w_hi[:, s, :], raw[:, r, :], ACT.Copy).then_inc(split_hi, 1)

            def tile_done(name, b, k, n, units, t):
                if t < NT - 1:
                    act.wait_ge(S[name], at(name, b, k))
                else:
                    act.wait_ge(unit_used, n + units)

            def norm(a, n, u, i, only=None):
                def square(t):
                    if i == 1:
                        act.wait_ge(S["out_added"], at("out_added", a, 4 + t + 1))
                    else:
                        act.wait_ge(x_loaded[t], a * 16 + 16)
                    nc.scalar.activation(xs[:, t, :], x_a[:, t, :], ACT.Square,
                                         accum_out=ss[:, t:t + 1]).then_inc(S["sq_done"], 1)

                def scale(t):
                    act.wait_ge(S["rstd_done"], at("rstd_done", a, 4 * i + t + 1))
                    nc.scalar.activation(xs[:, t, :], x_a[:, t, :], ACT.Copy,
                                         scale=rstd[:, t:t + 1]).then_inc(S["xs_ready"], 1)

                if first_block(a):
                    for t in range(NT):
                        square(t)
                    if i == 0:
                        for k in range(RAW):
                            split(0, 0, k - RING)
                    return
                if i == 0 and only == 0:
                    act.wait_ge(S["spread_done"], at("spread_done", a - 1, 4))
                if only is not None:
                    square(only)
                    scale(only)
                    return
                for t in range(NT):
                    square(t)
                    if t:
                        scale(t - 1)
                scale(NT - 1)

            def turn(a, n, u, i):
                if first_block(a) and i == 0:
                    act.wait_ge(vectors_read, 1)
                for dt in range(KT):
                    act.wait_ge(S["turned"], at("turned", a, 8 * i + dt + 1))
                    nc.scalar.activation(hT_hi[:, dt, :], ps[:, TURN_BANK[i][dt // 4] + dt % 4, :], ACT.Copy,
                                         scale=gain[i][:, dt:dt + 1]).then_inc(S["hT_hi_done"], 1)
                if not first_block(a):
                    for k in range(-1 - i, 0):
                        split(n, u, k)
                elif i == 0:
                    for k in range(RAW, RING):
                        split(0, 0, k - RING)

            def pool_in(a, n, u):
                if first_block(a):
                    act.wait_ge(const_ready, CONST_READY)
                else:
                    act.wait_ge(S["g_ready"], at("g_ready", a - 1, FT))
                    act.wait_ge(S["halo_kept"], at("halo_kept", a - 1, FT))
                for g in range(4):
                    split(n, u, g)
                    pool_copy(a, n, g)

            def pool_copy(a, n, g):
                act.wait_ge(unit_used, n + (g + 1))
                buf, bank = pbuf[:, g, :], ps[:, POOL_BANK + g, :]
                nc.scalar.activation(buf[:, 0:CARRY], p_keep[:, g, :], ACT.Copy).then_inc(S["p_carried"], 1)
                nc.scalar.activation(buf[:, CARRY:], bank, ACT.Copy)
                act.wait_ge(S["p_carried"], at("p_carried", a, g + 1))
                nc.scalar.activation(p_keep[:, g, :], bank[:, T - CARRY:T], ACT.Copy).then_inc(S["p_copied"], 1)

            def pool_map(a, n, u, g):
                act.wait_ge(S["pool_done"], at("pool_done", a, g + 1))
                nc.scalar.activation(mf[:, g, :], ps[:, POOL_BANK + g, :], ACT.Identity,
                                     bias=pbias[:, g:g + 1], scale=pscale[:, g:g + 1]
                                     ).then_inc(S["m_copied"], 1)

            def q_in(a, n, u, k0, k1):
                for k in range(k1 - k0 - (k1 == 4)):
                    split(n, u, k)
                if k1 < 4:
                    return
                for t in range(NT):
                    tile_done("q_done", a, t + 1, n, k1 - k0, t)
                    nc.scalar.activation(xs[:, t, 0:QC], ps[:, banks(first_block(a))[0] + t, :], ACT.Square
                                         ).then_inc(S["q_squared"], 1)
                split(n, u, k1 - k0 - 1)

            def kv_in(a, n, u, k0, k1):
                if k0 == 0:
                    return split(n, u, 0)
                act.wait_ge(S["v_kept"], at("v_kept", a, 1))
                for r in range(2):
                    if r == 0:
                        act.wait_ge(S["kv_done"], at("kv_done", a, 1))
                    else:
                        act.wait_ge(unit_used, n + 1)
                    kv = ps[:, banks(first_block(a))[1] + r, :].rearrange("p (t s n) -> p t s n", t=2, s=2)
                    k_in, v_in, t = kv[:, :, 0, :], kv[:, :, 1, :], 2 * r
                    nc.scalar.activation(v_odd[:, t:t + 2, :], v_in, ACT.Copy)
                    nc.scalar.activation(v_even[0:HD, t:t + 2, :], v_in[0:HD], ACT.Copy)
                    nc.scalar.activation(v_even[HD:P, t + 1:t + 3, :], v_in[HD:P], ACT.Copy)
                    nc.scalar.activation(xs[:, t:t + 2, QC:QC + KVC], k_in, ACT.Square
                                         ).then_inc(S["k_squared"], 1)
                split(n, u, 0)

            def k_turn(a, n, u):
                act.wait_ge(S["kT_done"], at("kT_done", a, 1))
                nc.scalar.activation(kT[:, 0, 0, 1], k_keep[:], ACT.Copy).then_inc(S["k_placed"], 1)
                by_chunk = ps[:, banks(first_block(a))[2], :].rearrange("p (t c d) -> p t c d", t=NT, c=2)
                even, odd = by_chunk[:, :, 0, :], by_chunk[:, :, 1, :]
                for dst, src in [(kT[:, :, 0, 0], even), (kT[:, :, 1, 0], even), (kT[:, :, 1, 1], odd),
                                 (kT[:, 1:NT, 0, 1], odd[:, 0:NT - 1])]:
                    nc.scalar.activation(dst, src, ACT.Copy, scale=gk[:, 0:1])
                act.wait_ge(S["k_placed"], at("k_placed", a, 1))
                nc.scalar.activation(k_keep[:], odd[:, NT - 1], ACT.Copy, scale=gk[:, 0:1]
                                     ).then_inc(S["kT_ready"], 1)

            def q_turn(a, n, u):
                for t in range(NT):
                    act.wait_ge(S["qT_done"], at("qT_done", a, t + 1))
                    nc.scalar.activation(qT[:, t, :], ps[:, Q_TURN_BANK + t, :], ACT.Copy,
                                         scale=gq[:, 0:1]).then_inc(S["qT_ready"], 1)

            def exps(a, t):
                act.wait_ge(S["shift_ready"], at("shift_ready", a, t + 1))
                nc.scalar.activation(sink_exp[:, t, :], sink_exp[:, t, :], ACT.Exp)
                for i in range(8):
                    ex = nc.scalar.activation(
                        xs[:, t, i * P:(i + 1) * P],
                        ps[:, SCORE_BANK[t] + i // 4, (i % 4) * P:(i % 4 + 1) * P], ACT.Exp,
                        bias=shift[:, t, i:i + 1], accum_out=row_sum[:, t, i:i + 1])
                ex.then_inc(S["exp_done"], 1)

            def scores(a, n, u, t):
                if t < 2:
                    exps(a, t)

            def spread(a, n, u, t):
                act.wait_ge(S["spread_done"], at("spread_done", a, t + 1))
                if t >= 2:
                    act.wait_ge(S["mix_done"], at("mix_done", a, t - 1))
                bank = SCORE_BANK[t]
                nc.scalar.activation(PT[:, t % 2].rearrange("p v c q -> p v (c q)"), ps[:, bank:bank + 2, :],
                                     ACT.Copy).then_inc(S["PT_ready"], 1)

            def mix(a, n, u, t):
                act.wait_ge(S["mix_done"], at("mix_done", a, t + 1))
                nc.scalar.activation(hT_hi[:, 0:4, t * P:(t + 1) * P],
                                     ps[:, SCORE_BANK[t], :].rearrange("p (j q) -> p j q", j=4),
                                     ACT.Copy).then_inc(S["aT_hi_done"], 1)
                if t == 1:
                    exps(a, 2)
                    exps(a, 3)

            def out_proj(a, n, u, h, k0, k1):
                for k in range(k1 - k0):
                    split(n, u, k)

            def up(b, n, u, f0, count):
                with act.Fori(0, count // 2) as j:
                    for i in range(2):
                        f = j * 2 + (f0 + i)
                        bank = UP_BANK[f0] + 2 * i
                        split(n + j * 4, u, 2 * i)
                        split(n + j * 4, u, 2 * i + 1)
                        act.wait_ge(S["g_ready"], at("g_ready", b, f - 1))
                        nc.scalar.activation(ub[:, i, :, 2:2 + T], ps[:, bank:bank + 2, :], ACT.Copy)
                        for s in range(2):
                            col = bass.ds(f + s * FT, 1)
                            cv = nc.scalar.activation(cb[:, i, s, :], ps[:, bank + s, :], ACT.Identity,
                                                      bias=cbias[:, col], scale=cw[2][:, col])
                        cv.then_inc(S["u_copied"], 1)
                        act.wait_ge(S["conv_done"], at("conv_done", b, f + 1))
                        act.wait_ge(S["halo_kept"], at("halo_kept", b, f + 1))
                        nc.scalar.activation(ub[:, i, 0, 2:2 + T], cb[:, i, 0, :], ACT.Tanh, scale=0.5
                                             ).then_inc(S["tanh_done"], 1)

            def down(b, n, u, g, h, k0, k1):
                for k in range(k1 - k0 - deferred(b, g, h)):
                    split(n, u, k)

            def store(b, n, u):
                for t in range(NT):
                    act.wait_ge(S["y_added"], at("y_added", b, 28 + t + 1))
                    act.dma_start(out_v[:, bass.ds(b * NT + t, 1), :], res[:, t:t + 1, :]
                                  ).then_inc(S["stored"], 16)

            act.sem_inc(S["u_copied"], START["u_copied"])
            act.sem_inc(S["stored"], START["stored"])
            walk(act, stages_of(norm=norm, turn=turn, pool_in=pool_in, pool_map=pool_map, q_in=q_in, kv_in=kv_in, q_turn=q_turn, k_turn=k_turn,
                                scores=scores, spread=spread, mix=mix, out=out_proj, up=up, down=down,
                                store=store))
            act.wait_ge(S["stored"], at("stored", NB - 1, 16 * NT))

        @block.vector
        def _(dve):
            v = nc.vector

            def split(n, u, k):
                m, r, s = k + RING, (u + k + RING) % RAW, (u + k + RING) % RING
                if isinstance(n, int) and n + m >= N_ALL:
                    return
                dve.wait_ge(split_hi, n + (m + 1))
                v.tensor_tensor(w_lo[:, s, :], raw[:, r, :], as_f32(w_hi[:, s, :]), ALU.subtract
                                ).then_inc(split_lo, 1)

            def tile_done(name, b, k, n, units, t):
                if t < NT - 1:
                    dve.wait_ge(S[name], at(name, b, k))
                else:
                    dve.wait_ge(unit_used, n + units)

            def norm(a, n, u, i, only=None):
                if not first_block(a):
                    return
                for t in range(NT):
                    if i == 0 and t == 2:
                        dve.wait_ge(const_turned, 1)
                        v.tensor_copy(cst[:], ps[:, 0, 0:200]).then_inc(vectors_read, 1)
                    dve.wait_ge(S["rstd_done"], at("rstd_done", a, 4 * i + t + 1))
                    v.tensor_scalar(xs[:, t, :], x_a[:, t, :], rstd[:, t:t + 1], None, ALU.mult
                                    ).then_inc(S["xs_ready"], 1)
                if i == 0:
                    for k in range(RAW):
                        split(0, 0, k - RING)

            def turn(a, n, u, i):
                for dt in range(KT):
                    dve.wait_ge(S["hT_hi_done"], at("hT_hi_done", a, 8 * i + dt + 1))
                    v.scalar_tensor_tensor(hT_lo[:, dt, :], ps[:, TURN_BANK[i][dt // 4] + dt % 4, :],
                                           gain[i][:, dt:dt + 1], as_f32(hT_hi[:, dt, :]),
                                           ALU.mult, ALU.subtract).then_inc(S["hT_lo_done"], 1)
                if not first_block(a):
                    for k in range(-1 - i, 0):
                        split(n, u, k)
                elif i == 0:
                    for k in range(RAW, RING):
                        split(0, 0, k - RING)
                    constants()

            STEP0 = (0, 3, 7, 12)

            def window(a, g):
                dve.wait_ge(S["p_copied"], at("p_copied", a, g + 1))
                step, p_g = STEP0[g], pbuf[:, g, :]
                src, lag = p_g, 1
                for k in range(g + 1):
                    lo = 2 * lag - 1
                    dst = sums[:, k % 2, :]
                    v.tensor_tensor(dst[:, lo:], src[:, lo:], src[:, lo - lag:T + CARRY - lag], ALU.add
                                    ).then_inc(S["win_step"], 1)
                    step += 1
                    dve.wait_ge(S["win_step"], at("win_step", a, step))
                    src, lag = dst, 2 * lag
                if first_block(a):
                    v.tensor_tensor(src[:, CARRY:2 * CARRY], src[:, CARRY:2 * CARRY], ratio[:, g, :], ALU.mult
                                    ).then_inc(const_step, 1)
                    dve.wait_ge(const_step, CONST_STEP + g + 1)
                v.scalar_tensor_tensor(p_g[:, CARRY:], src[:, CARRY:], 1.0 / WINDOWS[g], p_g[:, CARRY:],
                                       ALU.mult, ALU.subtract).then_inc(S["win_step"], 1)
                step += 1
                if g >= MIX:
                    dve.wait_ge(S["pool_done"], at("pool_done", a, g - MIX + 1))
                dve.wait_ge(S["win_step"], at("win_step", a, step))
                v.tensor_copy(mix_hi[:, g % MIX, :], p_g[:, CARRY:]).then_inc(S["win_step"], 1)

            def window_end(a, g):
                dve.wait_ge(S["win_step"], at("win_step", a, STEP0[g] + g + 3))
                v.tensor_tensor(mix_lo[:, g % MIX, :], pbuf[:, g, CARRY:], as_f32(mix_hi[:, g % MIX, :]), ALU.subtract
                                ).then_inc(S["mix_ready"], 1)

            def pool_in(a, n, u):
                for g in range(4):
                    split(n, u, g)
                    if g > 0:
                        window(a, g - 1)
                        window_end(a, g - 1)
                window(a, 3)
                window_end(a, 3)

            def q_in(a, n, u, k0, k1):
                for k in range(k1 - k0 - (k1 == 4)):
                    split(n, u, k)
                if k1 < 4:
                    return

                def summed(t):
                    dve.wait_ge(S["q_squared"], at("q_squared", a, t + 1))
                    v.tensor_reduce(ss_q[:, t, :], xs[:, t, 0:QC].rearrange("p (h d) -> p h d", h=8),
                                    AX.X, ALU.add).then_inc(S["q_summed"], 1)

                def scaled(t):
                    dve.wait_ge(S["q_rstd"], at("q_rstd", a, t + 1))
                    v.tensor_tensor(xs[:, t, 0:QC].rearrange("p (j v d) -> p v j d", v=2, j=4),
                                    ps[:, banks(first_block(a))[0] + t, :].rearrange("p (v j d) -> p v j d", v=2, j=4),
                                    rs_q[:, t, :].rearrange("p (v j) -> p v j", v=2).unsqueeze(3)
                                    .broadcast_to([P, 2, 4, HD]), ALU.mult
                                    ).then_inc(S["q_scaled"], 1)

                for t in range(NT):
                    summed(t)
                    if t:
                        scaled(t - 1)
                scaled(NT - 1)
                split(n, u, k1 - k0 - 1)

            def kv_in(a, n, u, k0, k1):
                if k0 == 0:
                    return split(n, u, 0)

                def pair(ap):
                    return ap.rearrange("p t (h d) -> p t h d", h=2)

                def k_of(r):
                    return xs[:, 2 * r:2 * r + 2, QC:QC + KVC]

                for r in range(2):
                    dve.wait_ge(S["k_squared"], at("k_squared", a, r + 1))
                    v.tensor_reduce(ss_k[:, 2 * r:2 * r + 2, :], pair(k_of(r)), AX.X, ALU.add
                                    ).then_inc(S["k_summed"], 1)
                for r in range(2):
                    dve.wait_ge(S["k_rstd"], at("k_rstd", a, r + 1))
                    k_in = ps[:, banks(first_block(a))[1] + r, :].rearrange("p (t s n) -> p t s n", t=2, s=2)[:, :, 0, :]
                    v.tensor_tensor(pair(k_of(r)), pair(k_in),
                                    rs_k[:, 2 * r:2 * r + 2, :].unsqueeze(3).broadcast_to([P, 2, 2, HD]), ALU.mult
                                    ).then_inc(S["k_scaled"], 1)
                split(n, u, 0)

            def join(a, n, u):
                dve.wait_ge(unit_used, n)
                dve.wait_ge(S["m_copied"], at("m_copied", a, 4))
                for g in range(4):
                    v.tensor_copy(hT_hi[:, 4 + g, :], mf[:, g, :]).then_inc(S["mT_step"], 1)
                for g in range(4):
                    dve.wait_ge(S["mT_step"], at("mT_step", a, g + 1))
                    v.tensor_tensor(hT_lo[:, 4 + g, :], mf[:, g, :], as_f32(hT_hi[:, 4 + g, :]), ALU.subtract
                                    ).then_inc(S["mT_ready"], 1)

            def inverse(a, t):
                dve.wait_ge(S["exp_done"], at("exp_done", a, t + 1))
                v.tensor_tensor(row_sum[:, t, :], row_sum[:, t, :], sink_exp[:, t, :], ALU.add
                                ).then_inc(S["sm_step"], 1)
                dve.wait_ge(S["sm_step"], at("sm_step", a, SM_INV[t]))
                v.reciprocal(row_sum[:, t, :], row_sum[:, t, :]).then_inc(S["inv_ready"], 1)

            SM_S, SM_INV = (0, 2, 6, 8), (5, 6, 11, 12)

            def scores(a, n, u, t):
                bank = SCORE_BANK[t]
                dve.wait_ge(S["score_done"], at("score_done", a, t + 1))
                if first_block(a) and t == 0:
                    for h in range(2):
                        v.memset(ps[:, bank + h, 0:2 * P].rearrange("p (j c k) -> p j c k", j=2, c=2)[:, :, 1, :],
                                 NEG).then_inc(const_step, 1)
                    dve.wait_ge(const_step, CONST_STEP + 6)
                v.tensor_reduce(mx[:, t, :].rearrange("p (v i) -> p v i", v=2),
                                ps[:, bank:bank + 2, :].rearrange("p v (i k) -> p v i k", i=4),
                                AX.X, ALU.max).then_inc(S["sm_step"], 1)
                dve.wait_ge(S["sm_step"], at("sm_step", a, SM_S[t] + 1))
                v.scalar_tensor_tensor(shift[:, t, :], mx[:, t, :], -1.0, neg_sink[:], ALU.mult, ALU.min
                                       ).then_inc(S["sm_step"], 1)
                dve.wait_ge(S["sm_step"], at("sm_step", a, SM_S[t] + 2))
                v.tensor_tensor(sink_exp[:, t, :], sink[:], shift[:, t, :], ALU.add
                                ).then_inc(S["shift_ready"], 1)
                if t == 1:
                    inverse(a, 0)
                    inverse(a, 1)
            def mix(a, n, u, t):
                dve.wait_ge(S["aT_hi_done"], at("aT_hi_done", a, t + 1))
                v.tensor_tensor(hT_lo[:, 0:4, t * P:(t + 1) * P],
                                ps[:, SCORE_BANK[t], :].rearrange("p (j q) -> p j q", j=4),
                                as_f32(hT_hi[:, 0:4, t * P:(t + 1) * P]), ALU.subtract
                                ).then_inc(S["aT_lo_done"], 1)
                if t == 1:
                    inverse(a, 2)
                    inverse(a, 3)

            def out_proj(a, n, u, h, k0, k1):
                for k in range(k1 - k0 - (k1 == 4)):
                    split(n, u, k)
                if k1 < 4:
                    return
                for t in range(NT):
                    tile_done("out_done", a, 3 * h + t + 1, n, k1 - k0, t)
                    c = slice(h * 512, (h + 1) * 512)
                    v.tensor_tensor(x_a[:, t, c], ps[:, OUT_BANK[h] + t, :], x_a[:, t, c], ALU.add
                                    ).then_inc(S["out_added"], 1)
                split(n, u, k1 - k0 - 1)

            def up(b, n, u, f0, count):
                with dve.Fori(0, count // 2) as j:
                    for i in range(2):
                        f = j * 2 + (f0 + i)
                        split(n + j * 4, u, 2 * i)
                        split(n + j * 4, u, 2 * i + 1)
                        dve.wait_ge(S["u_copied"], at("u_copied", b, f + 1))
                        dve.wait_ge(S["halo_in"], at("halo_in", b, f + 1))
                        for tap in (1, 0):
                            for s in range(2):
                                if tap == 0:
                                    dve.wait_ge(S["conv_step"], at("conv_step", b, f * 2 + (s + 1)))
                                st = v.scalar_tensor_tensor(cb[:, i, s, :], ub[:, i, s, tap:tap + T],
                                                            cw[tap][:, bass.ds(f + s * FT, 1)],
                                                            cb[:, i, s, :], ALU.mult, ALU.add)
                                if tap == 1:
                                    st.then_inc(S["conv_step"], 1)
                        st.then_inc(S["conv_done"], 1)
                        gate, value = cb[:, i, 0, :], cb[:, i, 1, :]
                        dve.wait_ge(S["tanh_done"], at("tanh_done", b, f + 1))
                        v.scalar_tensor_tensor(gate, ub[:, i, 0, 2:2 + T], 1.0, gate, ALU.add, ALU.mult
                                               ).then_inc(S["silu_step"], 1)
                        dve.wait_ge(S["silu_step"], at("silu_step", b, f * 3 + 1))
                        v.scalar_tensor_tensor(value, gate, 0.5, value, ALU.mult, ALU.mult
                                               ).then_inc(S["silu_step"], 1)
                        dve.wait_ge(S["silu_step"], at("silu_step", b, f * 3 + 2))
                        g_slot = bass.ds(j * 2 + i, 1)
                        v.tensor_copy(g_hi[:, g_slot, :], value.unsqueeze(1)).then_inc(S["silu_step"], 1)
                        dve.wait_ge(S["silu_step"], at("silu_step", b, f * 3 + 3))
                        v.tensor_tensor(g_lo[:, g_slot, :], value.unsqueeze(1), as_f32(g_hi[:, g_slot, :]),
                                        ALU.subtract).then_inc(S["g_ready"], 1)

            def down(b, n, u, g, h, k0, k1):
                if (g, h) == (0, 0):
                    dve.wait_ge(S["out_added"], at("out_added", b, 8))
                    dve.wait_ge(S["stored"], at("stored", b - 1, 16 * NT))
                    v.tensor_copy(res[:], x_a[:]).then_inc(S["res_copied"], 1)
                    dve.wait_ge(S["res_copied"], at("res_copied", b, 1))
                last = k1 == GROUPS[g] // 2
                late = deferred(b, g, h)
                for k in range(k1 - k0 - max(last, late)):
                    split(n, u, k)
                if not last:
                    return
                for t in range(NT):
                    tile_done("down_done", b, 3 * (2 * g + h) + t + 1, n, k1 - k0, t)
                    c = slice(h * 512, (h + 1) * 512)
                    v.tensor_tensor(res[:, t, c], ps[:, DOWN_BANK[g, h] + t, :], res[:, t, c], ALU.add
                                    ).then_inc(S["y_added"], 1)
                if not late:
                    split(n, u, k1 - k0 - 1)

            def constants():
                dve.wait_ge(const_in, CONST_IN)
                sink_of = sink_row[:].rearrange("p (v j i) -> p i v j", v=2, j=2)
                for i in range(2):
                    half = slice(i * HD, (i + 1) * HD)
                    for c in range(2):
                        v.tensor_copy(sink[half, :].rearrange("p (v c j) -> p c v j", v=2, c=2)[:, c],
                                      sink_of[half, i]).then_inc(const_step, 1)
                v.tensor_copy(pw_hi[:], pw_in).then_inc(const_step, 1)
                v.tensor_scalar(gk[:], gk_in[:], HD ** -0.5, None, ALU.mult).then_inc(const_ready, 1)
                dve.wait_ge(const_step, CONST_STEP)
                dve.wait_ge(vectors_read, 1)
                v.tensor_scalar(neg_sink[:], sink[:], -1.0, None, ALU.mult).then_inc(const_ready, 1)
                v.tensor_tensor(pw_lo[:], pw_in, as_f32(pw_hi[:]), ALU.subtract).then_inc(const_ready, 1)
                v.tensor_tensor(pbias[:], pbias_in, pscale, ALU.mult).then_inc(const_ready, 1)
                dve.wait_ge(const_pool, CONST_POOL)

            dve.sem_inc(S["g_ready"], START["g_ready"])
            walk(dve, stages_of(norm=norm, turn=turn, pool_in=pool_in, q_in=q_in, kv_in=kv_in,
                                join=join, scores=scores, mix=mix, out=out_proj, up=up, down=down))

        @block.gpsimd
        def _(pool):
            g = nc.gpsimd

            def wait(semaphore, value):
                pool.wait_ge(semaphore, value)
                if not isinstance(value, int):
                    pool.sem_inc(pool_waited, 1)

            def inverse_root(dst, src, count, width, step, k_step, done):
                g.tensor_scalar(dst, src, 1.0 / width, EPS, ALU.mult, ALU.add).then_inc(S[step], 1)
                wait(S[step], k_step)
                g.tensor_tensor(dst, dst, half_neg[:, 0:count], ALU.pow).then_inc(S[done], 1)

            def norm(a, n, u, i, only=None):
                for t in range(NT) if only is None else (only,):
                    wait(S["sq_done"], at("sq_done", a, 4 * i + t + 1))
                    inverse_root(rstd[:, t:t + 1], ss[:, t:t + 1], 1, D, "rstd_step",
                                 at("rstd_step", a, 4 * i + t + 1), "rstd_done")
                if i == 0 and only in (None, 0):
                    if not first_block(a):
                        wait(S["mix_done"], at("mix_done", a - 1, 4))
                    g.tensor_copy(v_even[:, 0, :], v_even[:, NT, :]).then_inc(S["v_kept"], 1)

            def q_in(a, n, u, k0, k1):
                for t in range(NT) if k1 == 4 else ():
                    wait(S["q_summed"], at("q_summed", a, t + 1))
                    inverse_root(rs_q[:, t, :], ss_q[:, t, :], 8, HD, "q_step", at("q_step", a, t + 1), "q_rstd")

            def kv_in(a, n, u, k0, k1):
                if k0 == 0:
                    return
                for r in range(2):
                    wait(S["k_summed"], at("k_summed", a, r + 1))
                    inverse_root(rs_k[:, 2 * r:2 * r + 2, :].rearrange("p t h -> p (t h)"),
                                 ss_k[:, 2 * r:2 * r + 2, :].rearrange("p t h -> p (t h)"),
                                 4, HD, "k_step", at("k_step", a, r + 1), "k_rstd")

            def scale_probs(a, t):
                wait(S["inv_ready"], at("inv_ready", a, t + 1))
                pr = xs[:, t, :].rearrange("p (i k) -> p i k", i=8)
                g.tensor_tensor(pr, pr, row_sum[:, t, :].unsqueeze(2).broadcast_to([P, 8, P]), ALU.mult
                                ).then_inc(S["p_scaled"], 1)

            def scores(a, n, u, t):
                if t == 1:
                    scale_probs(a, 0)
                    scale_probs(a, 1)
                if t == 3:
                    scale_probs(a, 2)

            def mix(a, n, u, t):
                if t == 1:
                    scale_probs(a, 3)

            def up(b, n, u, f0, count):
                with pool.Fori(0, count // 2) as j:
                    for i in range(2):
                        f = j * 2 + (f0 + i)
                        wait(S["g_ready"], at("g_ready", b, f - 1))
                        g.tensor_copy(ub[:, i, :, 0:2], halo[:, bass.ds(f, 1), :, :].squeeze(1)
                                      ).then_inc(S["halo_in"], 1)
                        wait(S["u_copied"], at("u_copied", b, f + 1))
                        wait(S["halo_in"], at("halo_in", b, f + 1))
                        g.tensor_copy(halo[:, bass.ds(f, 1), :, :].squeeze(1), ub[:, i, :, T:T + 2]
                                      ).then_inc(S["halo_kept"], 1)

            g.memset(ident[:], 0.0).then_inc(const_cleared, 1)
            g.memset(ratio[:], 1.0).then_inc(const_cleared, 1)
            wait(const_cleared, 2)
            g.affine_select(out=ident[:], in_=ident[:], compare_op=ALU.not_equal, fill=1.0, base=0,
                            pattern=[[-1, P]], channel_multiplier=1).then_inc(const_pool, 1)
            for i, w in enumerate(WINDOWS):
                for pos in range(w - 1):
                    ms = g.memset(ratio[:, i, pos:pos + 1], float(w) / (pos + 1))
            ms.then_inc(const_pool, 1)
            g.memset(half_neg[:], -0.5).then_inc(const_pool, 1)
            for ap in (k_keep[:], v_even[:], p_keep[:], halo[:]):
                g.memset(ap, 0.0).then_inc(const_pool, 1)
            wait(const_pool, CONST_POOL)
            walk(pool, stages_of(norm=norm, q_in=q_in, kv_in=kv_in, scores=scores, mix=mix, up=up))


_INS = ["x", "norm1_g", "w_in", "q_norm_g", "k_norm_g", "attn_sinks", "pool_w", "pool_b", "pool_scale",
        "w_out", "norm2_g", "w_up", "conv_w", "conv_b", "w_down"]
_OUTS = [((1, SEQ, D), "float32")]


def kernel(**inputs):
    import numpy as _np
    import concourse.bacc as _bacc
    from concourse import mybir as _mybir
    from concourse.bass_utils import run_bass_kernel_spmd as _run

    nc = _bacc.Bacc("TRN2", target_bir_lowering=False, num_devices=1)
    arrays, args = {}, []
    for name in _INS:
        a = _np.ascontiguousarray(inputs[name])
        arrays[f"in_{name}_dram"] = a
        args.append(nc.dram_tensor(f"in_{name}_dram", a.shape, _mybir.dt.from_np(a.dtype), kind="ExternalInput").ap())
    for i, (shape, dtype) in enumerate(_OUTS):
        dt = _mybir.dt.from_np(_np.dtype(dtype))
        args.append(nc.dram_tensor(f"out_{i}_dram", shape, dt, kind="ExternalOutput").ap())
    bass_hybrid_block(nc, *args)
    r = _run(nc, [arrays], core_ids=[0])
    got = tuple(r.results[0][f"out_{i}_dram"] for i in range(len(_OUTS)))
    return got[0]
```
